# Optimizing a Trainium2 kernel written in Bass

```python
import math
import jax
import jax.numpy as jnp
from jax import lax
import numpy as np

D_MODEL = 1024
BATCH = 1
SEQ = 512
DEPTH = 1
DEC_BATCH = 8
DEC_SEQ = 4
PAST_LEN = 1024
PAGE_SIZE = 128

A_HEADS = 8
A_DK = 128
A_DV = 128
A_CHUNK = 32
B_HEADS = 8
B_KV_HEADS = 2
B_HEAD_DIM = 128
B_GROUP = B_HEADS // B_KV_HEADS
IDX_HEADS = 4
IDX_DIM = 64
TOPK_MAX = 256
Q_BLOCK = 64
N_BUCKETS = 32
MAX_DISTANCE = 128
PEER_HEADS = 8
N_KEYS = 128
N_EXPERTS = N_KEYS * N_KEYS
PEER_DKEY = 256
PEER_HALF = PEER_DKEY // 2
PEER_TOPK = 16
PEER_BLOCK = 256
ALPHA = (2.0 * DEPTH) ** 0.25
BETA = (8.0 * DEPTH) ** -0.25
LN_EPS = 1e-5
RMS_EPS = 1e-6
IN_SIZES = (A_HEADS * A_DK, A_HEADS * A_DK, A_HEADS * A_DV, A_HEADS * A_DV,
            B_HEADS * B_HEAD_DIM, B_KV_HEADS * B_HEAD_DIM, B_KV_HEADS * B_HEAD_DIM,
            IDX_HEADS * IDX_DIM, IDX_DIM, IDX_HEADS, D_MODEL, D_MODEL)
IN_WIDTH = sum(IN_SIZES)

kernel_name = 'hybrid_hgrn2_dsa_peer_step'

F32 = jnp.float32

def layer_norm(x, g, b):
    xf = x.astype(F32)
    mu = xf.mean(-1, keepdims=True)
    var = jnp.square(xf - mu).mean(-1, keepdims=True)
    return ((xf - mu) * lax.rsqrt(var + LN_EPS) * g.astype(F32) + b.astype(F32)).astype(x.dtype)

def t5_bucket(rel):
    max_exact = N_BUCKETS // 2
    relf = jnp.maximum(rel, 1).astype(F32)
    large = max_exact + (jnp.log(relf / max_exact) / math.log(MAX_DISTANCE / max_exact)
                         * (N_BUCKETS - max_exact)).astype(jnp.int32)
    large = jnp.minimum(large, N_BUCKETS - 1)
    return jnp.where(rel < max_exact, rel, large)

def take_rows(a, idx):
    return jax.vmap(lambda ab, ib: ab[ib])(a, idx)

def hgrn2_recurrence(q, logf, v, s0):
    B, T = q.shape[:2]
    chunk = math.gcd(T, A_CHUNK)
    nc = T // chunk

    def to_chunks(a):
        return a.reshape(B, nc, chunk, A_HEADS, a.shape[-1]).transpose(1, 0, 3, 2, 4)

    qc, fc, vc = to_chunks(q), to_chunks(logf), to_chunks(v)
    mask = jnp.tril(jnp.ones((chunk, chunk), dtype=bool))

    def step(S, inp):
        qb, lf, vb = inp
        qb, lf, vb = qb.astype(F32), lf.astype(F32), vb.astype(F32)
        bcum = jnp.cumsum(lf, axis=2)
        blast = bcum[:, :, -1:, :]
        k = -jnp.expm1(lf)
        qe = qb * jnp.exp(bcum)
        ke = k * jnp.exp(-bcum)
        kd = k * jnp.exp(blast - bcum)
        scores = jnp.where(mask, jnp.einsum('bhtk,bhsk->bhts', qe, ke), 0.0)
        o = (jnp.einsum('bhtk,bhkv->bhtv', qe, S)
             + jnp.einsum('bhts,bhsv->bhtv', scores, vb))
        S_new = jnp.exp(blast)[:, :, 0, :, None] * S + jnp.einsum('bhsk,bhsv->bhkv', kd, vb)
        return S_new, o

    S, o = lax.scan(step, s0.astype(F32), (qc, fc, vc))
    o = o.transpose(1, 0, 3, 2, 4).reshape(B, T, A_HEADS, A_DV)
    return o, S.astype(s0.dtype)

def sparse_attention(q, qi, wi, q_pos, kidx_all, gather_kv, t5_table):
    B, T = q.shape[:2]
    L = kidx_all.shape[1]
    k_sel = min(TOPK_MAX, L // 4)
    blk = math.gcd(T, Q_BLOCK)
    nb = T // blk
    key_pos = jnp.arange(L, dtype=jnp.int32)
    kif = kidx_all.astype(F32)

    def to_blocks(a):
        return a.reshape((B, nb, blk) + a.shape[2:]).swapaxes(0, 1)

    def one_block(args):
        qb, qib, wib, pb = args
        s = jax.nn.relu(jnp.einsum('bthd,bsd->bths', qib.astype(F32), kif) * IDX_DIM ** -0.5)
        score = jnp.einsum('bths,bth->bts', s, wib.astype(F32)) * IDX_HEADS ** -0.5
        score = jnp.where((key_pos[None, :] <= pb[:, None])[None], score, -jnp.inf)
        vals, idx = lax.top_k(score, k_sel)
        valid = jnp.isfinite(vals)
        kg, vg = gather_kv(idx)
        qg = qb.reshape(B, blk, B_KV_HEADS, B_GROUP, B_HEAD_DIM).astype(F32)
        logits = jnp.einsum('btgrd,btkgd->btgrk', qg, kg.astype(F32)) * B_HEAD_DIM ** -0.5
        rel = jnp.maximum(pb[None, :, None] - idx, 0)
        bias = t5_table[t5_bucket(rel)].astype(F32)
        bias = bias.reshape(B, blk, k_sel, B_KV_HEADS, B_GROUP).transpose(0, 1, 3, 4, 2)
        logits = jnp.where(valid[:, :, None, None, :], logits + bias, -jnp.inf)
        p = jax.nn.softmax(logits, axis=-1)
        o = jnp.einsum('btgrk,btkgd->btgrd', p, vg.astype(F32))
        return o.reshape(B, blk, B_HEADS * B_HEAD_DIM).astype(q.dtype)

    out = lax.map(one_block, (to_blocks(q), to_blocks(qi), to_blocks(wi), q_pos.reshape(nb, blk)))
    return out.swapaxes(0, 1).reshape(B, T, B_HEADS * B_HEAD_DIM)

def peer_ffn(h, w_q, sub_keys, u_tab, v_tab):
    B, T, D = h.shape
    n = B * T
    nb = -(-n // PEER_BLOCK)
    hp = jnp.pad(h.reshape(n, D), ((0, nb * PEER_BLOCK - n), (0, 0))).reshape(nb, PEER_BLOCK, D)

    def one_block(xb):
        q = (xb @ w_q).reshape(PEER_BLOCK, PEER_HEADS, 2, PEER_HALF).astype(F32)
        s = jnp.einsum('nhcd,ckd->nhck', q, sub_keys.astype(F32))
        s1, i1 = lax.top_k(s[:, :, 0], PEER_TOPK)
        s2, i2 = lax.top_k(s[:, :, 1], PEER_TOPK)
        cand = (s1[..., :, None] + s2[..., None, :]).reshape(PEER_BLOCK, PEER_HEADS, PEER_TOPK * PEER_TOPK)
        cid = (i1[..., :, None] * N_KEYS + i2[..., None, :]).reshape(PEER_BLOCK, PEER_HEADS, PEER_TOPK * PEER_TOPK)
        top, pos = lax.top_k(cand, PEER_TOPK)
        eid = jnp.take_along_axis(cid, pos, axis=-1)
        g = jax.nn.softmax(top, axis=-1)
        act = jax.nn.gelu(jnp.einsum('nhed,nd->nhe', u_tab[eid].astype(F32), xb.astype(F32)),
                          approximate=False)
        out = jnp.einsum('nhe,nhed->nd', g * act, v_tab[eid].astype(F32))
        return out.astype(h.dtype)

    return lax.map(one_block, hp).reshape(nb * PEER_BLOCK, D)[:n].reshape(B, T, D)

def decoder_layer(x, c, s0, q_pos, key_source, layer_idx, w_ada, b_ada, w_in, lb_param, a_gnorm,
                  t5_table, w_out, ln1_g, ln1_b, w_peer_q, peer_sub_keys, peer_u, peer_v,
                  ln2_g, ln2_b):
    B, T, _ = x.shape
    mod = jax.nn.silu(c) @ w_ada + b_ada
    sh1, sc1, g1, sh2, sc2, g2 = jnp.split(mod[:, None, :], 6, axis=-1)
    h = x * (1 + sc1) + sh1
    z = h @ w_in
    splits = [int(s) for s in np.cumsum(IN_SIZES)[:-1]]
    qa, fa, ia, ga, qb, kb, vb, qi, ki, wi, gate_a, gate_b = jnp.split(z, splits, axis=-1)

    lb = jnp.cumsum(jax.nn.softmax(lb_param.astype(F32), axis=0), axis=0)[layer_idx]
    logf = jnp.log(lb + (1.0 - lb) * jax.nn.sigmoid(fa.astype(F32)))
    oa, s_new = hgrn2_recurrence(jax.nn.silu(qa).reshape(B, T, A_HEADS, A_DK),
                                 logf.reshape(B, T, A_HEADS, A_DK),
                                 ia.reshape(B, T, A_HEADS, A_DV), s0)
    oa = oa * lax.rsqrt(jnp.mean(jnp.square(oa), axis=-1, keepdims=True) + RMS_EPS) * a_gnorm.astype(F32)
    oa = (oa.reshape(B, T, A_HEADS * A_DV) * jax.nn.silu(ga.astype(F32))).astype(x.dtype)

    kb = kb.reshape(B, T, B_KV_HEADS, B_HEAD_DIM)
    vb = vb.reshape(B, T, B_KV_HEADS, B_HEAD_DIM)
    kidx_all, gather_kv = key_source(kb, vb, ki)
    ob = sparse_attention(qb.reshape(B, T, B_HEADS, B_HEAD_DIM), qi.reshape(B, T, IDX_HEADS, IDX_DIM),
                          wi, q_pos, kidx_all, gather_kv, t5_table)

    merged = jax.nn.sigmoid(gate_a) * oa + jax.nn.sigmoid(gate_b) * ob
    x = layer_norm(ALPHA * x + g1 * (merged @ w_out), ln1_g, ln1_b)
    h2 = x * (1 + sc2) + sh2
    x = layer_norm(ALPHA * x + g2 * peer_ffn(h2, w_peer_q, peer_sub_keys, peer_u, peer_v), ln2_g, ln2_b)
    return x, kb, vb, ki, s_new

def setup_inputs(seed: int = 0) -> dict:
    key = jax.random.key(seed)
    ks = jax.random.split(key, 24)
    n_pages = PAST_LEN // PAGE_SIZE
    n_used = DEC_BATCH * n_pages
    n_pool = n_used + max(1, n_used // 4)

    def nrm(k, shape, s):
        return jax.random.normal(k, shape, F32) * s

    return {
        'x_prompt': nrm(ks[0], (BATCH, SEQ, D_MODEL), 1.0),
        'x_sample': nrm(ks[1], (DEC_BATCH, DEC_SEQ, D_MODEL), 1.0),
        'cache_k': nrm(ks[2], (DEPTH, n_pool, PAGE_SIZE, B_KV_HEADS, B_HEAD_DIM), 1.0),
        'cache_v': nrm(ks[3], (DEPTH, n_pool, PAGE_SIZE, B_KV_HEADS, B_HEAD_DIM), 1.0),
        'cache_kidx': nrm(ks[4], (DEPTH, n_pool, PAGE_SIZE, IDX_DIM), 1.0),
        'state_hgrn': nrm(ks[5], (DEPTH, DEC_BATCH, A_HEADS, A_DK, A_DV), 0.5),
        'page_table': jax.random.permutation(ks[6], n_pool)[:n_used].reshape(DEC_BATCH, n_pages).astype(jnp.int32),
        'c_prompt': nrm(ks[7], (BATCH, D_MODEL), 1.0),
        'c_sample': nrm(ks[8], (DEC_BATCH, D_MODEL), 1.0),
        'w_ada': nrm(ks[9], (DEPTH, D_MODEL, 6 * D_MODEL), 0.5 * D_MODEL ** -0.5),
        'b_ada': nrm(ks[10], (DEPTH, 6 * D_MODEL), 0.02),
        'w_in': nrm(ks[11], (DEPTH, D_MODEL, IN_WIDTH), D_MODEL ** -0.5),
        'lb_param': nrm(ks[12], (DEPTH + 1, A_HEADS * A_DK), 0.1),
        'a_gnorm': 1.0 + nrm(ks[13], (DEPTH, A_DV), 0.01),
        't5_table': nrm(ks[14], (N_BUCKETS, B_HEADS), 0.5),
        'w_out': nrm(ks[15], (DEPTH, D_MODEL, D_MODEL), BETA * D_MODEL ** -0.5),
        'ln1_g': 1.0 + nrm(ks[16], (DEPTH, D_MODEL), 0.01),
        'ln1_b': nrm(ks[17], (DEPTH, D_MODEL), 0.01),
        'w_peer_q': nrm(ks[18], (DEPTH, D_MODEL, PEER_HEADS * PEER_DKEY), D_MODEL ** -0.5),
        'peer_sub_keys': nrm(ks[19], (DEPTH, 2, N_KEYS, PEER_HALF), PEER_HALF ** -0.5),
        'peer_u': nrm(ks[20], (DEPTH, N_EXPERTS, D_MODEL), D_MODEL ** -0.5),
        'peer_v': nrm(ks[21], (DEPTH, N_EXPERTS, D_MODEL), BETA * PEER_HEADS ** -0.5),
        'ln2_g': 1.0 + nrm(ks[22], (DEPTH, D_MODEL), 0.01),
        'ln2_b': nrm(ks[23], (DEPTH, D_MODEL), 0.01),
    }

def reference(x_prompt, x_sample, cache_k, cache_v, cache_kidx, state_hgrn, page_table, c_prompt,
              c_sample, w_ada, b_ada, w_in, lb_param, a_gnorm, t5_table, w_out, ln1_g, ln1_b,
              w_peer_q, peer_sub_keys, peer_u, peer_v, ln2_g, ln2_b):
    past_len = page_table.shape[1] * PAGE_SIZE
    n_dec = page_table.shape[0]
    yp, ys = x_prompt, x_sample
    kp_l, vp_l, ip_l, sp_l, ks_l, vs_l, is_l, ss_l = [], [], [], [], [], [], [], []
    for l in range(DEPTH):
        wts = (w_ada[l], b_ada[l], w_in[l], lb_param, a_gnorm[l], t5_table, w_out[l], ln1_g[l],
               ln1_b[l], w_peer_q[l], peer_sub_keys[l], peer_u[l], peer_v[l], ln2_g[l], ln2_b[l])

        def prompt_keys(kb, vb, ki):
            return ki, (lambda idx: (take_rows(kb, idx), take_rows(vb, idx)))

        s0 = jnp.zeros((yp.shape[0], A_HEADS, A_DK, A_DV), x_prompt.dtype)
        yp, kp, vp, ip, sp = decoder_layer(yp, c_prompt, s0, jnp.arange(yp.shape[1], dtype=jnp.int32),
                                           prompt_keys, l, *wts)

        ck, cv, ci = cache_k[l], cache_v[l], cache_kidx[l]

        def sample_keys(kb, vb, ki):
            past_idx = ci[page_table].reshape(n_dec, past_len, IDX_DIM)
            kidx_all = jnp.concatenate([past_idx, ki], axis=1)

            def gather(idx):
                in_past = (idx < past_len)[..., None, None]
                pidx = jnp.minimum(idx, past_len - 1)
                page = jnp.take_along_axis(page_table, (pidx // PAGE_SIZE).reshape(n_dec, -1),
                                           axis=1).reshape(idx.shape)
                off = pidx % PAGE_SIZE
                nidx = jnp.clip(idx - past_len, 0, kb.shape[1] - 1)
                kg = jnp.where(in_past, ck[page, off], take_rows(kb, nidx))
                vg = jnp.where(in_past, cv[page, off], take_rows(vb, nidx))
                return kg, vg

            return kidx_all, gather

        ys, ksm, vsm, ism, ssm = decoder_layer(ys, c_sample, state_hgrn[l],
                                               past_len + jnp.arange(ys.shape[1], dtype=jnp.int32),
                                               sample_keys, l, *wts)
        kp_l.append(kp); vp_l.append(vp); ip_l.append(ip); sp_l.append(sp)
        ks_l.append(ksm); vs_l.append(vsm); is_l.append(ism); ss_l.append(ssm)

    k_prompt = jnp.stack(kp_l)
    v_prompt = jnp.stack(vp_l)
    kidx_prompt = jnp.stack(ip_l)
    s_prompt = jnp.stack(sp_l)
    k_sample = jnp.stack(ks_l)
    v_sample = jnp.stack(vs_l)
    kidx_sample = jnp.stack(is_l)
    s_sample = jnp.stack(ss_l)
    return (yp, ys, k_prompt, v_prompt, kidx_prompt, s_prompt, k_sample, v_sample, kidx_sample, s_sample)


_drawn_inputs = setup_inputs


def setup_inputs(seed=0):
    import zlib

    import numpy as np

    out = dict(_drawn_inputs(seed))
    spreads = {}
    factors = {'cache_k': 7.1,
     'cache_v': 5.857,
     'cache_kidx': 6.602,
     'a_gnorm': 200.0,
     't5_table': 8.0,
     'ln1_g': 138.899,
     'ln1_b': 144.477,
     'ln2_g': 174.883,
     'ln2_b': 184.655}
    for name, (base, spread) in spreads.items():
        noise = np.random.default_rng([zlib.crc32(name.encode()), seed]).standard_normal(out[name].shape)
        drawn = base * np.exp(spread * noise) if base else spread * noise
        out[name] = jnp.asarray(drawn.astype(out[name].dtype))
    for name, factor in factors.items():
        out[name] = (out[name] * factor).astype(out[name].dtype)
    return out
```

```python
import math
from contextlib import ExitStack

import numpy as np
import concourse.bass as bass
from concourse import mybir

F32 = mybir.dt.float32
U32 = mybir.dt.uint32
I32 = mybir.dt.int32
ALU = mybir.AluOpType
ACT = mybir.ActivationFunctionType
AX = mybir.AxisListType

P = 128
D = 1024
KD = D // P
SEQ = 512
TILES = SEQ // P
NB, NS = 8, 4
ST = NB * NS
N = SEQ + ST
PAST, PAGE = 1024, 128
PAGES = PAST // PAGE
H = 8
GQ = 4
CH = 32
NCH = SEQ // CH
IH, ID = 4, 64
KSEL_P, KSEL_S = 128, 256
TW = PAST + ST
ALPHA = 2.0 ** 0.25
NEG = -1e30
MARK = -3e38
COLS = {"qa": 0, "fa": 1024, "ia": 2048, "ga": 3072, "qb": 4096, "kv": 5120, "ix": 5632, "gate_a": 5956, "gate_b": 6980}
WIN = 8004
SH1, SC1, G1, SH2, SC2, G2 = range(6)
PH, PK, TOPK = 8, 128, 16
GROUP = 4
UR, VR = 8, 12


def dap(ap, offset, pattern):
    return bass.AP(ap.tensor, ap.offset + offset, pattern)


def constants():
    def bucket(rel):
        rel = np.maximum(rel, 0)
        relf = np.maximum(rel, 1).astype(np.float32)
        large = 16 + (np.log(relf / np.float32(16)) / np.float32(math.log(8)) * np.float32(16)).astype(np.int32)
        return np.where(rel < 16, rel, np.minimum(large, 31))
    c = {}
    c["ident"] = np.eye(P)
    c["meanmat"] = np.full((P, P), 1.0 / P)
    s, t = np.arange(CH)[:, None], np.arange(CH)[None]
    tri = (s <= t)
    own = (s // NS == t // NS)
    big = np.arange(P)
    c["chunkmask"] = (big[:, None] <= big[None]) & (big[:, None] // CH == big[None] // CH)
    c["seqmask"] = tri & own
    c["ownchunk"] = big[:, None] // CH == np.arange(P // CH)[None]
    keep = np.ones(N)
    keep[0:SEQ:CH] = 0
    keep[SEQ::NS] = 0
    c["keep"] = np.tile(keep, (P, 1))
    c["ownseq"] = np.repeat((np.arange(ST)[:, None] // NS == np.arange(NB)[None]), 1, 1)
    c["causal"] = np.where(np.arange(P)[None] <= np.arange(P)[:, None], 0, NEG)
    c["newmask"] = np.where(tri.T & own.T, 0, NEG)
    c["t5p"] = (np.arange(32)[:, None] == bucket(511 - np.arange(640))[None])
    key = np.concatenate([np.arange(PAST), PAST + np.arange(ST) % NS])
    oh = [(np.arange(32)[:, None] == bucket(PAST + i - key)[None]) for i in range(NS)]
    c["t5s"] = np.concatenate(oh, 0)
    row = np.arange(P)
    c["rowq"] = (row[:, None] // 32 == (row[None] // GQ) % NS)
    c["expand"] = (np.arange(ST)[:, None] == row[None] // GQ)
    c["fold"] = (row[:, None] % ST == np.arange(ST)[None])
    c["iota16"] = np.tile(np.arange(TOPK), (P, 1))
    c["iotap"] = row[:, None]
    return {k: np.ascontiguousarray(v.astype(np.float32)) for k, v in c.items()}


class Counts:
    def __init__(self, eng, chain):
        self.eng, self.chain, self.n = eng, chain, {}

    def step(self, ins, sem=None):
        sem = sem or self.chain
        key = id(sem)
        self.n[key] = self.n.get(key, 0) + 1
        ins.then_inc(sem, 1)
        self.eng.wait_ge(sem, self.n[key])


def program(nc, a, o):
    es = ExitStack()
    live = []

    def sb(name, shape, dt, at):
        t = nc.alloc_sbuf_tensor_at(name, shape, dt, offset=at)
        return t

    stores = {name: nc.alloc_semaphore(name) for name in ("p_out", "r_out0", "r_out1", "e_out")}

    def sem(name):
        if name in stores:
            return stores[name]
        live.append(nc.alloc_semaphore(name))
        return live[-1]

    def next_stage():
        nc.clear_and_free_semaphores(live)
        nc.all_engine_barrier()
        live.clear()

    BASE = 16512
    cur = [BASE]

    def place(name, shape, dt=F32):
        at = cur[0]
        cur[0] += -(-int(np.prod(shape[1:])) * 4 // 32) * 32
        assert cur[0] <= 229344, (name, cur[0])
        return sb(name, shape, dt, at)

    PS = es.enter_context(nc.psum_tensor("PS", [P, 8 * 512], F32))

    def bank(i, w=512, p=P, off=0):
        return PS[0:p, 512 * i + off:512 * i + off + w]

    mod_d = nc.dram_tensor("mod_d", [1 + NB, 6 * D], F32, kind="Internal").ap()
    t5_d = nc.dram_tensor("t5_d", [H, 640], F32, kind="Internal").ap()
    t5x_d = nc.dram_tensor("t5x_d", [P, H, 640], F32, kind="Internal").ap()
    h2s_d = nc.dram_tensor("h2s_d", [ST, D], F32, kind="Internal").ap()

    ident = place("ident", [P, P])
    base_a = cur[0]
    q_s = place("q_s", [P, H, N])
    sn_s = place("sn_s", [P, H, N])
    v_s = place("v_s", [P, TILES + 1, D])
    base_b = cur[0]
    mg_s = place("mg_s", [P, H, N])
    gb_s = place("gb_s", [P, H, N])
    qb_s = place("qb_s", [P, H, N])
    kv_s = place("kv_s", [P, TILES + 1, 512])
    qi_s = place("qi_s", [ID, IH, N])
    ki_s = place("ki_s", [ID, N])
    kw_s = place("kw_s", [P, TILES + 1, ID + IH])
    base_c = cur[0]
    hT = place("hT", [P, KD, N])
    base_d = cur[0]

    cur[0] = base_a
    WR = 3
    c9 = place("c9", [1 + NB, D])
    cT = place("cT", [P, KD, 1 + NB])
    bada = place("bada", [1 + NB, 6 * D])
    modr = place("modr", [1 + NB, 6 * D])
    modT = place("modT", [P, 2 * KD, 1 + NB])
    xt = place("xt", [P, TILES + 1, D])
    htmp = place("htmp", [P, ST])
    w_ada_b = place("w_ada_b", [P, WR, KD, 512])
    assert cur[0] <= base_c, (cur[0], base_c)
    s_c, s_x, s_id, s_ba = sem("s_c"), sem("s_x"), sem("s_id"), sem("s_ba")
    s_wa = [sem(f"s_wa{i}") for i in range(WR)]
    m_ct, m_ctready, m_ps, m_row, m_tr, m_xt, m_h, m_chain, m_out = (sem(f"m_{k}") for k in
        ("ct", "ctready", "ps", "row", "tr", "xt", "h", "chain", "out"))
    m_modT = sem("m_modT")
    with nc.Block() as block:
        @block.sync
        def _(sp):
            sp.dma_start(ident[:, :], a["ident"]).then_inc(s_id, 16)
            sp.dma_start(c9[0:1, :], a["c_prompt"]).then_inc(s_c, 16)
            sp.dma_start(c9[1:1 + NB, :], a["c_sample"]).then_inc(s_c, 16)
            sp.dma_start(bada[:, :], dap(a["b_ada"], 0, [[0, 1 + NB], [1, 6 * D]])).then_inc(s_ba, 16)
            for n in range(12):
                if n >= WR:
                    sp.wait_ge(m_ps, n - WR + 1)
                src = dap(a["w_ada"], n * 512, [[6 * D, P], [P * 6 * D, KD], [1, 512]])
                sp.dma_start(w_ada_b[:, n % WR, :, :], src).then_inc(s_wa[n % WR], 16)
            sp.wait_ge(m_row, 12)
            sp.dma_start(mod_d, modr[:, :]).then_inc(m_out, 16)
            sp.wait_ge(m_out, 16)

        @block.gpsimd
        def _(pool):
            pool.dma_start(xt[:, 0:TILES, :], dap(a["x_prompt"], 0, [[D, P], [P * D, TILES], [1, D]])).then_inc(s_x, 16)
            pool.dma_start(xt[0:ST, TILES, :], dap(a["x_sample"], 0, [[D, ST], [1, D]])).then_inc(s_x, 16)
            pool.wait_ge(s_x, 32)

        @block.tensor
        def _(pe):
            pe.wait_ge(s_id, 16)
            pe.wait_ge(s_c, 32)
            for k in range(KD):
                last = nc.tensor.transpose(bank(0, 9, P, 16 * k), c9[:, P * k:P * k + P], ident[0:9, 0:9])
            last.then_inc(m_ct, 1)
            pe.wait_ge(m_ctready, 1)
            for n in range(12):
                pe.wait_ge(s_wa[n % WR], 16 * (n // WR + 1))
                if n >= 2:
                    pe.wait_ge(m_row, n - 1)
                for k in range(KD):
                    last = nc.tensor.matmul(bank(1 + n % 2, 512, 9), cT[:, k, :], w_ada_b[:, n % WR, k, :],
                                            start=k == 0, stop=k == KD - 1)
                last.then_inc(m_ps, 1)
                if n == 4:
                    for k in range(2 * KD):
                        pe.wait_ge(m_row, 4)
                        last = nc.tensor.transpose(bank(3, 9, P, 16 * k), modr[:, P * k:P * k + P], ident[0:9, 0:9])
                    last.then_inc(m_tr, 1)
                    pe.wait_ge(s_x, 32)
                    for k in range(KD):
                        if k >= 2:
                            pe.wait_ge(m_h, k - 1)
                        for t in range(TILES):
                            nc.tensor.transpose(bank(4 + k % 2, P, P, P * t), xt[:, t, P * k:P * k + P], ident[:, :])
                        nc.tensor.transpose(bank(6 + k % 2, ST), xt[0:ST, TILES, P * k:P * k + P],
                                            ident[0:ST, 0:ST]).then_inc(m_xt, 1)

        @block.scalar
        def _(act):
            act.wait_ge(m_ct, 1)
            for k in range(KD):
                last = nc.scalar.activation(cT[:, k, :], bank(0, 9, P, 16 * k), ACT.Silu)
            last.then_inc(m_ctready, 1)

        @block.vector
        def _(dve):
            c = Counts(dve, m_chain)
            dve.wait_ge(s_ba, 16)

            def row(n):
                dve.wait_ge(m_ps, n + 1)
                c.step(nc.vector.tensor_tensor(modr[:, 512 * n:512 * n + 512], bank(1 + n % 2, 512, 9),
                                               bada[:, 512 * n:512 * n + 512], ALU.add), m_row)
            for n in range(5):
                row(n)
            dve.wait_ge(m_tr, 1)
            src = bank(3, 256).rearrange("p (k c) -> p k c", c=16)[:, :, 0:9]
            c.step(nc.vector.tensor_copy(modT[:, :, :], src))
            c.step(nc.vector.tensor_scalar(modT[:, KD:2 * KD, :], modT[:, KD:2 * KD, :], 1.0, None, ALU.add))
            for k in range(KD):
                dve.wait_ge(m_xt, k + 1)
                c.step(nc.vector.tensor_scalar(hT[:, k, 0:SEQ], bank(4 + k % 2), modT[:, KD + k, 0:1],
                                               modT[:, k, 0:1], ALU.mult, ALU.add))
                seq3 = lambda ap: ap.rearrange("p (b i) -> p b i", i=NS)
                by_seq = lambda j: modT[:, j, 1:9].unsqueeze(2).to_broadcast([P, NB, NS])
                c.step(nc.vector.tensor_tensor(seq3(htmp[:, :]), seq3(bank(6 + k % 2, ST)), by_seq(KD + k), ALU.mult))
                c.step(nc.vector.tensor_tensor(seq3(hT[:, k, SEQ:N]), seq3(htmp[:, :]), by_seq(k), ALU.add), m_h)
            for n in range(5, 12):
                row(n)

    next_stage()
    cur[0] = base_d
    wb = place("wb", [P, WR, KD, 512])
    sg = place("sg", [P, 2, N])
    chunks = [("qa", 0, 512), ("qa", 512, 512), ("ga", 0, 512), ("ga", 512, 512), ("fa", 0, 512), ("fa", 512, 512),
              ("gate_a", 0, 512), ("gate_a", 512, 512), ("gate_b", 0, 512), ("gate_b", 512, 512),
              ("qb", 0, 512), ("qb", 512, 512), ("kv", 0, 512), ("ix", 0, 324), ("ia", 0, 512), ("ia", 512, 512)]
    units = []
    for n, (name, off, _) in enumerate(chunks):
        if name in ("kv", "ia"):
            units += [(n, name, t) for t in range(TILES + 1)]
        elif name == "ix":
            units += [(n, "qi", h) for h in range(IH)] + [(n, "ki", 0)] + [(n, "kw", t) for t in range(TILES + 1)]
        else:
            units += [(n, name, j) for j in range(4)]
    SLOTS = 4
    s_wb = [sem(f"s_wb{i}") for i in range(WR)]
    p_unit, p_chain, p_sg, p_sgused, p_out, p_achain = (sem(f"p_{k}") for k in
        ("unit", "chain", "sg", "sgused", "out", "achain"))
    p_free = [sem(f"p_free{i}") for i in range(SLOTS)]
    p_kvdone, p_kwdone = sem("p_kvdone"), sem("p_kwdone")
    with nc.Block() as block:
        @block.sync
        def _(sp):
            for n, (name, off, w) in enumerate(chunks):
                if n >= WR:
                    sp.wait_ge(p_unit, sum(1 for x in units if x[0] <= n - WR))
                src = dap(a["w_in"], COLS[name] + off, [[WIN, P], [P * WIN, KD], [1, w]])
                sp.dma_start(wb[:, n % WR, :, 0:w], src).then_inc(s_wb[n % WR], 16)
            sp.wait_ge(p_kvdone, TILES + 1)
            for j, (po, so) in enumerate((("k_prompt", "k_sample"), ("v_prompt", "v_sample"))):
                sp.dma_start(dap(o[po], 0, [[256, P], [P * 256, TILES], [1, 256]]),
                             kv_s[:, 0:TILES, 256 * j:256 * j + 256]).then_inc(p_out, 16)
                sp.dma_start(dap(o[so], 0, [[256, ST], [1, 256]]), kv_s[0:ST, TILES, 256 * j:256 * j + 256]).then_inc(p_out, 16)
            sp.wait_ge(p_kwdone, TILES + 1)
            sp.dma_start(dap(o["kidx_prompt"], 0, [[ID, P], [P * ID, TILES], [1, ID]]), kw_s[:, 0:TILES, 0:ID]).then_inc(p_out, 16)
            sp.dma_start(dap(o["kidx_sample"], 0, [[ID, ST], [1, ID]]), kw_s[0:ST, TILES, 0:ID]).then_inc(p_out, 16)
            sp.wait_ge(p_out, 96)

        @block.tensor
        def _(pe):
            seen = -1
            for u, (n, kind, j) in enumerate(units):
                if n != seen:
                    pe.wait_ge(s_wb[n % WR], 16 * (n // WR + 1))
                    seen = n
                if u >= SLOTS:
                    pe.wait_ge(p_free[u % SLOTS], u // SLOTS)
                b0 = 2 * (u % SLOTS)
                for k in range(KD):
                    w = wb[:, n % WR, k, :]
                    fl = dict(start=k == 0, stop=k == KD - 1)
                    if kind in ("kv", "ia", "kw"):
                        lo, m = P * j, P if j < TILES else ST
                        rhs = w[:, 256:256 + ID + IH] if kind == "kw" else w
                        last = nc.tensor.matmul(bank(b0, ID + IH if kind == "kw" else 512, m), hT[:, k, lo:lo + m], rhs, **fl)
                    else:
                        m = ID if kind in ("qi", "ki") else P
                        lo = 256 if kind == "ki" else m * j
                        nc.tensor.matmul(bank(b0, SEQ, m), w[:, lo:lo + m], hT[:, k, 0:SEQ], **fl)
                        last = nc.tensor.matmul(bank(b0 + 1, ST, m), w[:, lo:lo + m], hT[:, k, SEQ:N], **fl)
                last.then_inc(p_unit, 1)

        def src(u, p=P, w=N):
            b0 = 2 * (u % SLOTS)
            return PS[0:p, 512 * b0:512 * b0 + w]

        @block.scalar
        def _(act):
            c = Counts(act, p_achain)
            for u, (n, kind, j) in enumerate(units):
                if kind not in ("qa", "ga", "fa", "gate_a", "gate_b"):
                    continue
                h = 4 * (chunks[n][1] // 512) + j
                act.wait_ge(p_unit, u + 1)
                free = p_free[u % SLOTS]
                if kind == "qa":
                    nc.scalar.activation(q_s[:, h, :], src(u), ACT.Silu).then_inc(free, 1)
                elif kind == "ga":
                    nc.scalar.activation(mg_s[:, h, :], src(u), ACT.Silu).then_inc(free, 1)
                elif kind == "fa":
                    nc.scalar.activation(sn_s[:, h, :], src(u), ACT.Sigmoid, scale=-1.0).then_inc(free, 1)
                elif kind == "gate_b":
                    nc.scalar.activation(gb_s[:, h, :], src(u), ACT.Sigmoid).then_inc(free, 1)
                else:
                    if h >= 2:
                        act.wait_ge(p_sgused, h - 1)
                    nc.scalar.activation(sg[:, h % 2, :], src(u), ACT.Sigmoid).then_inc(p_sg, 1)
                    act.wait_ge(p_sg, h + 1)
                    act.sem_inc(free, 1)

        @block.vector
        def _(dve):
            c = Counts(dve, p_chain)
            for u, (n, kind, j) in enumerate(units):
                if kind in ("qa", "ga", "fa", "gate_b"):
                    continue
                half = chunks[n][1] // 512
                free = p_free[u % SLOTS]
                if kind == "gate_a":
                    h = 4 * half + j
                    dve.wait_ge(p_sg, h + 1)
                    nc.vector.tensor_tensor(mg_s[:, h, :], mg_s[:, h, :], sg[:, h % 2, :], ALU.mult).then_inc(p_sgused, 1)
                    continue
                dve.wait_ge(p_unit, u + 1)
                m = P if j < TILES else ST
                if kind == "qb":
                    nc.vector.tensor_scalar(qb_s[:, 4 * half + j, :], src(u), float(P) ** -0.5, None, ALU.mult).then_inc(free, 1)
                elif kind == "qi":
                    nc.vector.tensor_copy(qi_s[:, j, :], src(u, ID)).then_inc(free, 1)
                elif kind == "ki":
                    nc.vector.tensor_copy(ki_s[:, :], src(u, ID)).then_inc(free, 1)
                elif kind == "ia":
                    nc.vector.tensor_copy(v_s[0:m, j, 512 * half:512 * half + 512], src(u, m, 512)).then_inc(free, 1)
                elif kind == "kv":
                    c.step(nc.vector.tensor_copy(kv_s[0:m, j, :], src(u, m, 512)), p_kvdone)
                    dve.sem_inc(free, 1)
                elif kind == "kw":
                    c.step(nc.vector.tensor_copy(kw_s[0:m, j, :], src(u, m, ID + IH)), p_kwdone)
                    dve.sem_inc(free, 1)

    next_stage()
    cur[0] = base_c
    ab = place("ab", [P, 2, N])
    bc = place("bc", [P, 2, N])
    eb = place("eb", [P, 2, N])
    ke = place("ke", [P, 2, N])
    kd_t = place("kd_t", [P, 2, TILES + 1, P])
    scm = place("scm", [P, 2, SEQ + CH])
    st = place("st", [P, 2, NCH + 1, P])
    s0 = place("s0", [P, 2, NB, P])
    vm = place("vm", [ST, NB, P])
    sn_new = place("sn_new", [P, 2, NB, P])
    sq = place("sq", [P, N])
    rstd = place("rstd", [P, N])
    keep = place("keep", [P, N])
    cmask = place("cmask", [P, P])
    smask = place("smask", [ST, CH])
    ownchunk = place("ownchunk", [P, P // CH])
    vc = place("vc", [P, TILES, P // CH, P])
    ownseq = place("ownseq", [ST, NB])
    meanm = place("meanm", [P, P])
    lbp = place("lbp", [P, 2, H])
    lbm = place("lbm", [P, 3, H])
    gn = place("gn", [P, 1])
    eps6 = place("eps6", [P, 1])
    r_vc = sem("r_vc")
    r_lnms, r_rstd = sem("r_lnms"), sem("r_rstd")
    r_in, r_own, r_chain, r_sm, r_lb, r_ln, r_scan, r_exp, r_d, r_ed, r_prep, r_sc, r_scm, r_kdp, r_kdt, r_ds, r_st, r_dss, r_o, r_sq, r_ms, r_mg, r_vm, r_snew, r_ones = (
        sem(f"r_{k}") for k in ("in", "own", "chain", "sm", "lb", "ln", "scan", "exp", "d", "ed", "prep", "sc", "scm", "kdp", "kdt",
                                "ds", "st", "dss", "o", "sq", "ms", "mg", "vm", "snew", "ones"))
    r_s0 = [sem(f"r_s0{i}") for i in range(2)]
    r_out = [sem(f"r_out{i}") for i in range(2)]
    r_lbd = sem("r_lbd")
    chunks3 = lambda ap: ap[:, 0:SEQ].rearrange("p (c t) -> p c t", t=CH)
    seqs3 = lambda ap: ap[:, SEQ:N].rearrange("p (b t) -> p b t", t=NS)
    with nc.Block() as block:
        def store(sp, h):
            sp.wait_ge(r_st, NCH * (h + 1))
            sp.dma_start(dap(o["s_prompt"], h * P * P, [[P, P], [1, P]]), st[:, h % 2, NCH, :]).then_inc(r_out[h % 2], 16)
            sp.wait_ge(r_snew, 2 * (h + 1))
            sp.dma_start(dap(o["s_sample"], h * P * P, [[P, P], [H * P * P, NB], [1, P]]), sn_new[:, h % 2, :, :]).then_inc(r_out[h % 2], 16)

        @block.sync
        def _(sp):
            for dst, name in ((keep, "keep"), (cmask, "chunkmask"), (meanm, "meanmat"), (smask, "seqmask")):
                sp.dma_start(dst[:, :], a[name]).then_inc(r_in, 16)
            sp.dma_start(ownseq[:, :], a["ownseq"]).then_inc(r_own, 16)
            sp.dma_start(ownchunk[:, :], a["ownchunk"]).then_inc(r_own, 16)
            sp.dma_start(gn[:, :], dap(a["a_gnorm"], 0, [[1, P], [1, 1]])).then_inc(r_in, 16)
            for h in range(H):
                if h >= 2:
                    sp.wait_ge(r_mg, h - 1)
                    sp.wait_ge(r_snew, 2 * (h - 1))
                sp.dma_start(s0[:, h % 2, :, :], dap(a["state_hgrn"], h * P * P, [[P, P], [H * P * P, NB], [1, P]])).then_inc(r_s0[h % 2], 16)
                if h >= 1:
                    store(sp, h - 1)
            store(sp, H - 1)
            sp.wait_ge(r_out[0], 16 * H)
            sp.wait_ge(r_out[1], 16 * H)

        @block.gpsimd
        def _(pool):
            for j in range(2):
                pool.dma_start(lbp[:, j, :], dap(a["lb_param"], j * D, [[1, P], [P, H]]), allow_slow_non_contiguous=True).then_inc(r_lbd, 16)
            pool.wait_ge(r_own, 32)
            for h in range(H):
                for t in range(TILES):
                    if h >= 1:
                        pool.wait_ge(r_ds, TILES * (h - 1) + t + 1)
                    nc.gpsimd.tensor_tensor(vc[:, t, :, :], v_s[:, t, P * h:P * h + P].unsqueeze(1).to_broadcast([P, P // CH, P]),
                                            ownchunk[:, :].unsqueeze(2).to_broadcast([P, P // CH, P]), ALU.mult).then_inc(r_vc, 1)
                if h >= 1:
                    pool.wait_ge(r_dss, 2 * h)
                nc.gpsimd.tensor_tensor(vm[:, :, :], v_s[0:ST, TILES, P * h:P * h + P].unsqueeze(1).to_broadcast([ST, NB, P]),
                                        ownseq[:, :].unsqueeze(2).to_broadcast([ST, NB, P]), ALU.mult).then_inc(r_vm, 1)
            pool.wait_ge(r_lbd, 32)

        @block.scalar
        def _(act):
            act.wait_ge(r_sm, 1)
            nc.scalar.activation(lbm[:, 0:2, :], lbp[:, :, :], ACT.Exp).then_inc(r_lb, 1)
            act.wait_ge(r_ones, 1)

            def logs(h):
                if h >= 2:
                    act.wait_ge(r_kdt, h - 1)
                    act.wait_ge(r_mg, h - 1)
                i = h % 2
                nc.scalar.activation(ab[:, i, :], sn_s[:, h, :], ACT.Ln, scale=lbm[:, 2, h:h + 1], bias=1.0).then_inc(r_ln, 1)
                act.wait_ge(r_scan, h + 1)
                nc.scalar.activation(eb[:, i, :], bc[:, i, :], ACT.Exp).then_inc(r_exp, 1)
                nc.scalar.activation(ke[:, i, :], bc[:, i, :], ACT.Exp, scale=-1.0).then_inc(r_exp, 1)
                act.wait_ge(r_d, h + 1)
                nc.scalar.activation(ab[:, i, :], ab[:, i, :], ACT.Exp).then_inc(r_ed, 1)

            logs(0)
            for h in range(H):
                if h + 1 < H:
                    logs(h + 1)
                act.wait_ge(r_kdp, h + 1)
                if h >= 2:
                    act.wait_ge(r_dss, 2 * (h - 1))
                nc.scalar.activation(kd_t[:, h % 2, 0:TILES, :], bank(0).rearrange("p (t k) -> p t k", k=P), ACT.Copy).then_inc(r_kdt, 1)
                act.wait_ge(r_o, h + 1)
                nc.scalar.activation(sq[:, :], PS[:, 4 * 512:4 * 512 + N], ACT.Square).then_inc(r_sq, 1)
                act.wait_ge(r_ms, h + 1)
                if h >= 1:
                    act.wait_ge(r_mg, h)
                nc.scalar.activation(rstd[:, :], PS[:, 6 * 512:6 * 512 + N], ACT.Ln, bias=eps6[:, 0:1]).then_inc(r_lnms, 1)
                act.wait_ge(r_lnms, h + 1)
                nc.scalar.activation(rstd[:, :], rstd[:, :], ACT.Exp, scale=-0.5).then_inc(r_rstd, 1)

        @block.vector
        def _(dve):
            c = Counts(dve, r_chain)
            dve.wait_ge(r_in, 80)
            c.step(nc.vector.memset(eps6[:, :], 1e-6))
            dve.wait_ge(r_lbd, 32)
            c.step(nc.vector.tensor_tensor(lbm[:, 2, :], lbp[:, 0, :], lbp[:, 1, :], ALU.max))
            c.step(nc.vector.tensor_tensor(lbp[:, :, :], lbp[:, :, :], lbm[:, 2, :].unsqueeze(1).to_broadcast([P, 2, H]), ALU.subtract), r_sm)
            dve.wait_ge(r_lb, 1)
            c.step(nc.vector.tensor_tensor(lbm[:, 2, :], lbm[:, 0, :], lbm[:, 1, :], ALU.add))
            c.step(nc.vector.reciprocal(lbm[:, 2, :], lbm[:, 2, :]))
            c.step(nc.vector.tensor_tensor(lbm[:, 1, :], lbm[:, 1, :], lbm[:, 2, :], ALU.mult))
            c.step(nc.vector.tensor_scalar(lbm[:, 2, :], lbm[:, 1, :], -1.0, None, ALU.mult), r_ones)

            def prep(h):
                i = h % 2
                dve.wait_ge(r_ln, h + 1)
                nc.vector.tensor_scalar(sn_s[:, h, :], sn_s[:, h, :], lbm[:, 1, h:h + 1], None, ALU.mult)
                c.step(nc.vector.tensor_tensor_scan(bc[:, i, :], keep[:, :], ab[:, i, :], 0.0, ALU.mult, ALU.add), r_scan)
                c.step(nc.vector.tensor_tensor(chunks3(ab[:, i, :]), chunks3(bc[:, i, :])[:, :, CH - 1:CH].to_broadcast([P, NCH, CH]),
                                        chunks3(bc[:, i, :]), ALU.subtract))
                c.step(nc.vector.tensor_tensor(seqs3(ab[:, i, :]), seqs3(bc[:, i, :])[:, :, NS - 1:NS].to_broadcast([P, NB, NS]),
                                               seqs3(bc[:, i, :]), ALU.subtract), r_d)
                dve.wait_ge(r_exp, 2 * (h + 1))
                c.step(nc.vector.tensor_tensor(q_s[:, h, :], q_s[:, h, :], eb[:, i, :], ALU.mult))
                c.step(nc.vector.tensor_tensor(ke[:, i, :], ke[:, i, :], sn_s[:, h, :], ALU.mult))
                dve.wait_ge(r_ed, h + 1)
                c.step(nc.vector.tensor_tensor(ab[:, i, :], ab[:, i, :], sn_s[:, h, :], ALU.mult), r_prep)

            prep(0)
            for h in range(H):
                i = h % 2
                if h + 1 < H:
                    prep(h + 1)
                dve.wait_ge(r_sc, h + 1)
                shape = [P, TILES, P // CH, CH]
                c.step(nc.vector.tensor_tensor(scm[:, i, 0:SEQ].rearrange("p (t c s) -> p t c s", c=P // CH, s=CH),
                                               bank(1, P).rearrange("p (t s) -> p t s", s=CH).unsqueeze(2).to_broadcast(shape),
                                               cmask[:, :].rearrange("p (c s) -> p c s", s=CH).unsqueeze(1).to_broadcast(shape), ALU.mult))
                c.step(nc.vector.tensor_tensor(scm[0:ST, i, SEQ:SEQ + CH], bank(1, CH, ST, P), smask[:, :], ALU.mult))
                c.step(nc.vector.tensor_copy(kd_t[0:ST, i, TILES, :], bank(1, P, ST, 256)), r_scm)
                if h >= 2:
                    dve.wait_ge(r_out[i], 32 * (h // 2))
                for n in range(NCH):
                    t = n // 4
                    if n % 4 == 0:
                        dve.wait_ge(r_ds, TILES * h + t + 1)
                    ds = bank(2 + t % 2, P, P, P * (n % 4))
                    if n == 0:
                        c.step(nc.vector.tensor_copy(st[:, i, 1, :], ds), r_st)
                    else:
                        c.step(nc.vector.scalar_tensor_tensor(st[:, i, n + 1, :], st[:, i, n, :], eb[:, i, CH * n + CH - 1:CH * n + CH],
                                                              ds, ALU.mult, ALU.add), r_st)
                dve.wait_ge(r_s0[i], 16 * (h // 2 + 1))
                last = seqs3(eb[:, i, :])[:, :, NS - 1:NS].to_broadcast([P, NB, P])
                c.step(nc.vector.tensor_tensor(sn_new[:, i, :, :], s0[:, i, :, :], last, ALU.mult))
                for j in range(2):
                    dve.wait_ge(r_dss, 2 * h + j + 1)
                    c.step(nc.vector.tensor_tensor(sn_new[:, i, 4 * j:4 * j + 4, :], sn_new[:, i, 4 * j:4 * j + 4, :],
                                                   bank(2 + j).rearrange("p (b v) -> p b v", v=P), ALU.add), r_snew)
                dve.wait_ge(r_rstd, h + 1)
                c.step(nc.vector.tensor_tensor(rstd[:, :], rstd[:, :], PS[:, 4 * 512:4 * 512 + N], ALU.mult))
                c.step(nc.vector.scalar_tensor_tensor(mg_s[:, h, :], rstd[:, :], gn[:, 0:1], mg_s[:, h, :], ALU.mult, ALU.mult), r_mg)

        @block.tensor
        def _(pe):
            pe.wait_ge(r_in, 80)
            for h in range(H):
                i = h % 2
                v = lambda t, lo, n: v_s[lo:lo + n, t, P * h:P * h + P]
                pe.wait_ge(r_prep, h + 1)
                if h >= 1:
                    pe.wait_ge(r_scm, h)
                for n in range(NCH):
                    lo = 32 * (n % 4)
                    nc.tensor.matmul(PS[lo:lo + 32, 512 + CH * (n // 4):512 + CH * (n // 4) + CH], ke[:, i, CH * n:CH * n + CH],
                                     q_s[:, h, CH * n:CH * n + CH], start=True, stop=True)
                nc.tensor.matmul(bank(1, CH, ST, P), ke[:, i, SEQ:N], q_s[:, h, SEQ:N], start=True, stop=True)
                nc.tensor.transpose(bank(1, P, ST, 256), ab[:, i, SEQ:N], ident[:, :]).then_inc(r_sc, 1)
                if h >= 1:
                    pe.wait_ge(r_kdt, h)
                for t in range(TILES):
                    last = nc.tensor.transpose(bank(0, P, P, P * t), ab[:, i, P * t:P * t + P], ident[:, :])
                last.then_inc(r_kdp, 1)
                pe.wait_ge(r_kdt, h + 1)
                for t in range(TILES):
                    if t >= 2:
                        pe.wait_ge(r_st, NCH * h + 4 * (t - 1))
                    elif h >= 1:
                        pe.wait_ge(r_snew, 2 * h)
                    pe.wait_ge(r_vc, TILES * h + t + 1)
                    nc.tensor.matmul(bank(2 + t % 2), kd_t[:, i, t, :], vc[:, t, :, :], start=True, stop=True).then_inc(r_ds, 1)
                pe.wait_ge(r_vm, h + 1)
                pe.wait_ge(r_scm, h + 1)
                for j in range(2):
                    pe.wait_ge(r_st, NCH * h + 12 + 4 * j)
                    nc.tensor.matmul(bank(2 + j), kd_t[0:ST, i, TILES, :], vm[:, 4 * j:4 * j + 4, :], start=True, stop=True).then_inc(r_dss, 1)
                if h >= 1:
                    pe.wait_ge(r_mg, h)
                for t in range(TILES):
                    nc.tensor.matmul(bank(4, P, P, P * t), v(t, 0, P), scm[:, i, P * t:P * t + P], start=True, stop=False)
                    for n in range(max(4 * t, 1), 4 * t + 4):
                        nc.tensor.matmul(bank(4, CH, P, CH * n), st[:, i, n, :], q_s[:, h, CH * n:CH * n + CH], start=False,
                                         stop=n == 4 * t + 3)
                pe.wait_ge(r_s0[i], 16 * (h // 2 + 1))
                nc.tensor.matmul(bank(5, ST), v(TILES, 0, ST), scm[0:ST, i, SEQ:SEQ + CH], start=True, stop=False)
                for b in range(NB):
                    last = nc.tensor.matmul(bank(5, NS, P, NS * b), s0[:, i, b, :], q_s[:, h, SEQ + NS * b:SEQ + NS * b + NS],
                                            start=False, stop=b == NB - 1)
                last.then_inc(r_o, 1)
                pe.wait_ge(r_sq, h + 1)
                nc.tensor.matmul(bank(6), meanm[:, :], sq[:, 0:SEQ], start=True, stop=True)
                nc.tensor.matmul(bank(7, ST), meanm[:, :], sq[:, SEQ:N], start=True, stop=True).then_inc(r_ms, 1)

    next_stage()
    spans = []

    def fresh(name, shape, dt=F32):
        size = -(-int(np.prod(shape[1:])) * 4 // 32) * 32
        for s in spans:
            if s[0] + size <= s[1]:
                s[0] += size
                where[name] = s[0] - size
                return sb(name, shape, dt, s[0] - size)
        raise AssertionError((name, size, spans))

    where = {}
    spans[:] = [[base_a, base_b], [base_c, 229344]]
    KR = 3
    kvr = fresh("kvr", [P, KR, PAGES, 256])
    kT_c = fresh("kT_c", [P, 2, PAST])
    bt = fresh("bt", [P, H, SEQ])
    kxr = fresh("kxr", [P, 2, PAGES, ID])
    kxT = fresh("kxT", [ID, 2, PAST])
    t5s = fresh("t5s", [P, TW])
    selp = fresh("selp", [P, TILES, SEQ])
    work = fresh("work", [P, SEQ])
    rel = fresh("rel", [P, IH, TW // 2])
    rels = fresh("rels", [P, TW])
    sels = fresh("sels", [ST, TW])
    lg = fresh("lg", [P, 2, SEQ])
    pw = fresh("pw", [P, 2, SEQ])
    pT = fresh("pT", [P, 2, SEQ])
    qpad = fresh("qpad", [P, 2, NB, P])
    qall = fresh("qall", [P, 2, P])
    qipad = fresh("qipad", [ID, NB, IH, ST])
    qiall = fresh("qiall", [ID, P])
    kTp = fresh("kTp", [P, 2, N])
    pTs = sb("pTs", [P, 2, PAGES + 1, P], F32, where["bt"])
    ps_s = sb("ps_s", [P, 2, TW], F32, where["rel"])
    mtmp = fresh("mtmp", [P, GQ, P])
    causal = fresh("causal", [P, P])
    newmask = fresh("newmask", [ST, ST])
    rowq = fresh("rowq", [P, P])
    expand = fresh("expand", [ST, P])
    fold = fresh("fold", [P, ST])
    iotap = fresh("iotap", [P, 1])
    tab = fresh("tab", [P, H])
    t5row = fresh("t5row", [H, 640])
    t5p = fresh("t5p", [32, 640])
    ptab = fresh("ptab", [P, NB * PAGES], I32)
    ptabf = fresh("ptabf", [P, NB * PAGES])
    rows = fresh("rows", [P, NB * PAGES], I32)
    wcol = fresh("wcol", [P, 1])
    tbias = fresh("tbias", [P, 2, P])
    m8 = fresh("m8", [P, 8])
    mx = fresh("mx", [P, 2, 4])
    t_bt0 = sem("t_bt0")
    t_in, t_w, t_pt, t_rows, t_chain, t_row, t_t5, t_bt = (sem(f"t_{k}") for k in ("in", "w", "pt", "rows", "chain", "row", "t5", "bt"))
    t_pad0, t_pad, t_kn, t_knc, t_ix, t_rel, t_acc = (sem(f"t_{k}") for k in ("pad0", "pad", "kn", "knc", "ix", "rel", "acc"))
    t_kxt, t_kxc, t_xs, t_relS, t_relw, t_fold, t_sels = (sem(f"t_{k}") for k in ("kxt", "kxc", "xs", "relS", "relw", "fold", "sels"))
    t_lg, t_add, t_max, t_exp, t_norm, t_tr, t_pT, t_pv, t_merge = (sem(f"t_{k}") for k in
        ("lg", "add", "max", "exp", "norm", "tr", "pT", "pv", "merge"))
    t_kct, t_kcc, t_kcu, t_sl, t_smax, t_sexp, t_snorm, t_str, t_spT, t_spv, t_vu, t_smerge = (sem(f"t_{k}") for k in
        ("kct", "kcc", "kcu", "sl", "smax", "sexp", "snorm", "str", "spT", "spv", "vu", "smerge"))
    t_kx = [sem(f"t_kx{i}") for i in range(2)]
    t_kv = [sem(f"t_kv{i}") for i in range(KR)]
    widths = [P * (t + 1) for t in range(TILES)]
    heads = [(t, h) for t in range(TILES) for h in range(H)]
    SPAN = lambda b0, lo, hi, p=P: PS[0:p, 512 * b0 + lo:512 * b0 + hi]
    pieces = [(0, 512), (512, 1024), (1024, TW)]
    with nc.Block() as block:
        @block.sync
        def _(sp):
            sp.dma_start(ptab[:, :], dap(a["page_table"], 0, [[0, P], [1, NB * PAGES]])).then_inc(t_pt, 16)
            sp.dma_start(iotap[:, :], a["iotap"]).then_inc(t_pt, 16)
            for i in range(NS):
                sp.dma_start(tab[32 * i:32 * i + 32, :], a["t5_table"]).then_inc(t_in, 16)
            for i in range(IH):
                sp.dma_start(wcol[ST * i:ST * i + ST, :], kw_s[0:ST, TILES, ID + i:ID + i + 1]).then_inc(t_w, 16)
            for dst, name in ((t5p, "t5p"), (t5s, "t5s"), (causal, "causal"), (newmask, "newmask"), (rowq, "rowq"), (expand, "expand"), (fold, "fold")):
                sp.dma_start(dst[:, :], a[name]).then_inc(t_in, 16)
            sp.wait_ge(t_row, 2)
            sp.dma_start(t5_d, t5row[:, :]).then_inc(t_t5, 16)
            sp.wait_ge(t_t5, 16)
            sp.dma_start(t5x_d, dap(t5_d, 0, [[0, P], [640, H], [1, 640]])).then_inc(t_t5, 16)
            sp.wait_ge(t_t5, 32)
            sp.dma_start(bt[:, :, :], dap(t5x_d, P - 1, [[H * 640 - 1, P], [640, H], [1, SEQ]])).then_inc(t_bt, 16)
            sp.wait_ge(t_bt, 16)

        @block.gpsimd
        def _(pool):
            nc.gpsimd.memset(qpad[:, :, :, :], 0.0)
            nc.gpsimd.memset(qipad[:, :, :, :], 0.0).then_inc(t_pad0, 1)
            pool.wait_ge(t_rows, 1)
            gather = lambda dst, src, at, s: nc.gpsimd.indirect_dma_start(
                out=dst, out_offset=None, in_=src, in_offset=bass.IndirectOffsetOnAxis(rows[:, at:at + 1], 0)).then_inc(s, 16)
            flat = lambda name, w: dap(a[name], 0, [[w, 80 * PAGE], [1, w]])
            for b in range(NB):
                if b >= 2:
                    pool.wait_ge(t_kxt, b - 1)
                for g in range(PAGES):
                    gather(kxr[:, b % 2, g, :], flat("cache_kidx", ID), b * PAGES + g, t_kx[b % 2])
            for n in range(2 * NB):
                if KR <= n < NB + KR:
                    pool.wait_ge(t_kct, 2 * (n - KR + 1))
                elif n >= NB + KR:
                    pool.wait_ge(t_vu, n - KR - NB + 1)
                for g in range(PAGES):
                    gather(kvr[:, n % KR, g, :], flat("cache_k" if n < NB else "cache_v", 256), (n % NB) * PAGES + g, t_kv[n % KR])

        @block.tensor
        def _(pe):
            pe.wait_ge(t_in, 16 * 11)
            nc.tensor.matmul(bank(0, 512, H), tab[0:32, :], t5p[:, 0:512], start=True, stop=True)
            nc.tensor.matmul(bank(1, 128, H), tab[0:32, :], t5p[:, 512:640], start=True, stop=True).then_inc(t_bt0, 1)
            for g in range(2):
                for t in range(TILES):
                    nc.tensor.transpose(bank(2 + 2 * g, P, P, P * t), kv_s[:, t, P * g:P * g + P], ident[:, :])
                last = nc.tensor.transpose(bank(3 + 2 * g, ST), kv_s[0:ST, TILES, P * g:P * g + P], ident[0:ST, 0:ST])
            last.then_inc(t_kn, 1)
            for n, (t, h) in enumerate([(t, h) for t in range(1, TILES) for h in range(IH)]):
                if n >= 2:
                    pe.wait_ge(t_rel, n - 1)
                else:
                    pe.wait_ge(t_row, 2)
                nc.tensor.matmul(bank(n % 2, widths[t]), qi_s[:, h, P * t:P * t + P], ki_s[:, 0:widths[t]], start=True, stop=True).then_inc(t_ix, 1)
            pe.wait_ge(t_pad, 1)
            pe.wait_ge(t_knc, 2)
            pe.wait_ge(t_rel, 12)
            nc.tensor.matmul(SPAN(2, PAST, TW), qiall[:, :], ki_s[:, SEQ:N], start=True, stop=True)
            for b in range(NB):
                pe.wait_ge(t_kx[b % 2], 16 * PAGES * (b // 2 + 1))
                if b >= 1:
                    pe.wait_ge(t_kxc, b)
                for g in range(PAGES):
                    last = nc.tensor.transpose(SPAN(0, P * g, P * g + P, ID), kxr[:, b % 2, g, :], ident[:, :])
                last.then_inc(t_kxt, 1)
                pe.wait_ge(t_kxc, b + 1)
                for lo, hi in pieces[0:2]:
                    last = nc.tensor.matmul(SPAN(2, lo, hi), qipad[:, b, :, :], kxT[:, b % 2, lo:hi], start=b == 0, stop=b == NB - 1)
            last.then_inc(t_xs, 1)
            pe.wait_ge(t_relw, 1)
            for lo, hi in pieces:
                last = nc.tensor.matmul(SPAN(5, lo, hi, ST), fold[:, :], rels[:, lo:hi], start=True, stop=True)
            last.then_inc(t_fold, 1)

            def weighted(n):
                t, h = heads[n]
                pe.wait_ge(t_norm, n + 1)
                if n >= 2:
                    pe.wait_ge(t_pT, n - 1)
                for s in range(t + 1):
                    last = nc.tensor.transpose(bank(2 + n % 2, P, P, P * s), pw[:, n % 2, P * s:P * s + P], ident[:, :])
                last.then_inc(t_tr, 1)
                pe.wait_ge(t_pT, n + 1)
                if h % GQ == 0 and n >= 2 * GQ:
                    pe.wait_ge(t_merge, n // GQ - 1)
                for s in range(t + 1):
                    last = nc.tensor.matmul(bank(6 + (n // GQ) % 2, P, P, P * (h % GQ)), kv_s[:, s, 256 + P * (h // GQ):256 + P * (h // GQ) + P],
                                            pT[:, n % 2, P * s:P * s + P], start=s == 0, stop=s == t)
                last.then_inc(t_pv, 1)

            pe.wait_ge(t_sels, 1)
            for n, (t, h) in enumerate(heads):
                if n >= 2:
                    pe.wait_ge(t_add, n - 1)
                nc.tensor.matmul(bank(4 + n % 2, widths[t]), qb_s[:, h, P * t:P * t + P], kTp[:, h // GQ, 0:widths[t]],
                                 start=True, stop=True).then_inc(t_lg, 1)
                if n >= 1:
                    weighted(n - 1)
            weighted(len(heads) - 1)
            pe.wait_ge(t_merge, 2 * TILES)
            for g in range(2):
                for lo, hi in pieces:
                    nc.tensor.matmul(SPAN(2 + 3 * g, lo, hi), tbias[:, g, :], t5s[:, lo:hi], start=True, stop=False)
                nc.tensor.matmul(SPAN(2 + 3 * g, PAST, TW), qall[:, g, :], kTp[:, g, SEQ:N], start=False, stop=False)
            for b in range(NB):
                pe.wait_ge(t_kv[b % KR], 16 * PAGES * (b // KR + 1))
                for g in range(2):
                    if 2 * b + g >= 1:
                        pe.wait_ge(t_kcc, 2 * b + g)
                    for s in range(PAGES):
                        last = nc.tensor.transpose(SPAN(0, P * s, P * s + P), kvr[:, b % KR, s, P * g:P * g + P], ident[:, :])
                    last.then_inc(t_kct, 1)
                    pe.wait_ge(t_kcc, 2 * b + g + 1)
                    for lo, hi in pieces[0:2]:
                        last = nc.tensor.matmul(SPAN(2 + 3 * g, lo, hi), qpad[:, g, b, :], kT_c[:, g, lo:hi], start=False, stop=False)
                    last.then_inc(t_kcu, 1)
            for g in range(2):
                for lo, hi in pieces:
                    last = nc.tensor.matmul(SPAN(2 + 3 * g, lo, hi), expand[:, :], sels[:, lo:hi], start=False, stop=True)
                last.then_inc(t_sl, 1)
            pe.wait_ge(t_sexp, 2)
            for g in range(2):
                pe.wait_ge(t_snorm, g + 1)
                for s in range(PAGES):
                    nc.tensor.transpose(SPAN(3 * g, P * s, P * s + P), ps_s[:, g, P * s:P * s + P], ident[:, :])
                nc.tensor.transpose(SPAN(3 * g, PAST, PAST + P, ST), ps_s[:, g, PAST:TW], ident[:, :]).then_inc(t_str, 1)
                pe.wait_ge(t_spT, g + 1)
                nc.tensor.matmul(bank(6 + g, P), kv_s[0:ST, TILES, 256 + P * g:256 + P * g + P], pTs[0:ST, g, PAGES, :], start=True, stop=False)
            for b in range(NB):
                n = NB + b
                pe.wait_ge(t_kv[n % KR], 16 * PAGES * (n // KR + 1))
                for g in range(2):
                    for s in range(PAGES):
                        last = nc.tensor.matmul(bank(6 + g, 16, P, 16 * b), kvr[:, n % KR, s, P * g:P * g + P],
                                                pTs[:, g, s, 16 * b:16 * b + 16], start=False, stop=b == NB - 1 and s == PAGES - 1)
                last.then_inc(t_vu, 1)

        @block.scalar
        def _(act):
            for n, (t, h) in enumerate([(t, h) for t in range(1, TILES) for h in range(IH)]):
                act.wait_ge(t_ix, n + 1)
                if n >= IH:
                    act.wait_ge(t_acc, n - IH + 1)
                nc.scalar.activation(rel[:, h, 0:widths[t]], bank(n % 2, widths[t]), ACT.Relu, scale=ID ** -0.5).then_inc(t_rel, 1)
            for b in range(NB):
                act.wait_ge(t_kxt, b + 1)
                nc.scalar.activation(kxT[:, b % 2, :], SPAN(0, 0, PAST, ID), ACT.Copy).then_inc(t_kxc, 1)
            act.wait_ge(t_xs, 1)
            nc.scalar.activation(rels[:, :], SPAN(2, 0, TW), ACT.Relu, scale=ID ** -0.5).then_inc(t_relS, 1)

            def copy_out(n):
                t, h = heads[n]
                act.wait_ge(t_tr, n + 1)
                if n >= 2:
                    act.wait_ge(t_pv, n - 1)
                nc.scalar.activation(pT[:, n % 2, 0:widths[t]], bank(2 + n % 2, widths[t]), ACT.Copy).then_inc(t_pT, 1)

            for n, (t, h) in enumerate(heads):
                act.wait_ge(t_max, n + 1)
                if n >= 2:
                    act.wait_ge(t_tr, n - 1)
                nc.scalar.activation(pw[:, n % 2, 0:widths[t]], lg[:, n % 2, 0:widths[t]], ACT.Exp, bias=mx[:, n % 2, 1:2],
                                     accum_out=mx[:, n % 2, 2:3]).then_inc(t_exp, 1)
                if n >= 1:
                    copy_out(n - 1)
            copy_out(len(heads) - 1)
            for n in range(2 * NB):
                act.wait_ge(t_kct, n + 1)
                if n >= 2:
                    act.wait_ge(t_kcu, n - 1)
                nc.scalar.activation(kT_c[:, n % 2, :], SPAN(0, 0, PAST), ACT.Copy).then_inc(t_kcc, 1)
            for g in range(2):
                act.wait_ge(t_smax, g + 1)
                nc.scalar.activation(ps_s[:, g, :], SPAN(2 + 3 * g, 0, TW), ACT.Exp, bias=mx[:, g, 1:2], accum_out=mx[:, g, 2:3]).then_inc(t_sexp, 1)
            for g in range(2):
                act.wait_ge(t_str, g + 1)
                nc.scalar.activation(pTs[:, g, 0:PAGES, :], SPAN(3 * g, 0, PAST).rearrange("p (s r) -> p s r", r=P), ACT.Copy)
                nc.scalar.activation(pTs[0:ST, g, PAGES, :], SPAN(3 * g, PAST, PAST + P, ST), ACT.Copy).then_inc(t_spT, 1)

        @block.vector
        def _(dve):
            c = Counts(dve, t_chain)
            dve.wait_ge(t_pt, 32)
            c.step(nc.vector.tensor_copy(ptabf[:, :], ptab[:, :]))
            c.step(nc.vector.tensor_scalar(rows[:, :], ptabf[:, :], float(PAGE), iotap[:, 0:1], ALU.mult, ALU.add), t_rows)
            dve.wait_ge(t_bt0, 1)
            c.step(nc.vector.tensor_copy(t5row[:, 0:512], bank(0, 512, H)), t_row)
            c.step(nc.vector.tensor_copy(t5row[:, 512:640], bank(1, 128, H)), t_row)
            dve.wait_ge(t_kn, 1)
            for g in range(2):
                c.step(nc.vector.tensor_copy(kTp[:, g, :], SPAN(2 + 2 * g, 0, N)), t_knc)
            dve.wait_ge(t_pad0, 1)
            for b in range(NB):
                c.step(nc.vector.tensor_copy(qipad[:, b, :, NS * b:NS * b + NS], qi_s[:, :, SEQ + NS * b:SEQ + NS * b + NS]))
            c.step(nc.vector.tensor_copy(qiall[:, :].rearrange("p (h t) -> p h t", t=ST), qi_s[:, :, SEQ:N]), t_pad)
            qv = lambda g, b0, b1: qb_s[:, GQ * g:GQ * g + GQ, SEQ + NS * b0:SEQ + NS * b1].rearrange("p r t -> p t r")
            for g in range(2):
                c.step(nc.vector.tensor_copy(qall[:, g, :].rearrange("p (t r) -> p t r", r=GQ), qv(g, 0, NB)))
                for b in range(NB):
                    c.step(nc.vector.tensor_copy(qpad[:, g, b, 16 * b:16 * b + 16].rearrange("p (t r) -> p t r", r=GQ), qv(g, b, b + 1)))
                c.step(nc.vector.tensor_tensor(tbias[:, g, :].rearrange("p (t r) -> p t r", r=GQ), rowq[:, :].rearrange("p (t r) -> p t r", r=GQ),
                                               tab[:, GQ * g:GQ * g + GQ].unsqueeze(1).to_broadcast([P, ST, GQ]), ALU.mult))

            def take_top(w, k):
                for r in range(k // 8):
                    c.step(nc.vector.max(m8[0:w.shape[0], :], w))
                    c.step(nc.vector.match_replace(w, m8[0:w.shape[0], :], w, MARK))

            c.step(nc.vector.tensor_copy(selp[:, 0, 0:P], causal[:, :]))
            for t in range(1, TILES):
                w = work[:, 0:widths[t]]
                for h in range(IH):
                    n = IH * (t - 1) + h
                    wi = kw_s[:, t, ID + h:ID + h + 1]
                    dve.wait_ge(t_rel, n + 1)
                    if h == 0:
                        c.step(nc.vector.tensor_scalar(w, rel[:, h, 0:widths[t]], wi, None, ALU.mult), t_acc)
                    else:
                        c.step(nc.vector.scalar_tensor_tensor(w, rel[:, h, 0:widths[t]], wi, w, ALU.mult, ALU.add), t_acc)
                c.step(nc.vector.tensor_scalar(w, w, IH ** -0.5, None, ALU.mult))
                c.step(nc.vector.tensor_tensor(work[:, P * t:P * t + P], work[:, P * t:P * t + P], causal[:, :], ALU.add))
                take_top(w, KSEL_P)
                c.step(nc.vector.tensor_scalar(selp[:, t, 0:widths[t]], w, MARK, NEG, ALU.not_equal, ALU.mult))
            dve.wait_ge(t_relS, 1)
            dve.wait_ge(t_w, 16 * IH)
            c.step(nc.vector.tensor_scalar(rels[:, :], rels[:, :], wcol[:, 0:1], None, ALU.mult), t_relw)
            dve.wait_ge(t_fold, 1)
            c.step(nc.vector.tensor_scalar(sels[:, :], SPAN(5, 0, TW, ST), IH ** -0.5, None, ALU.mult))
            c.step(nc.vector.tensor_tensor(sels[:, PAST:TW], sels[:, PAST:TW], newmask[:, :], ALU.add))
            take_top(sels[:, :], KSEL_S)
            c.step(nc.vector.tensor_scalar(sels[:, :], sels[:, :], MARK, NEG, ALU.not_equal, ALU.mult), t_sels)

            def normalise(n):
                t, h = heads[n]
                dve.wait_ge(t_exp, n + 1)
                c.step(nc.vector.reciprocal(mx[:, n % 2, 3:4], mx[:, n % 2, 2:3]))
                c.step(nc.vector.tensor_scalar(pw[:, n % 2, 0:widths[t]], pw[:, n % 2, 0:widths[t]], mx[:, n % 2, 3:4], None, ALU.mult), t_norm)

            def merge(q):
                t, g = q // 2, q % 2
                dve.wait_ge(t_pv, GQ * (q + 1))
                c.step(nc.vector.tensor_tensor(mtmp[:, :, :], bank(6 + q % 2).rearrange("p (h t) -> p h t", t=P),
                                               gb_s[:, GQ * g:GQ * g + GQ, P * t:P * t + P], ALU.mult))
                m = mg_s[:, GQ * g:GQ * g + GQ, P * t:P * t + P]
                c.step(nc.vector.tensor_tensor(m, m, mtmp[:, :, :], ALU.add), t_merge)

            dve.wait_ge(t_bt, 16)
            for n, (t, h) in enumerate(heads):
                w = widths[t]
                i = n % 2
                dve.wait_ge(t_lg, n + 1)
                c.step(nc.vector.tensor_tensor(lg[:, i, 0:w], bank(4 + i, w), bt[:, h, SEQ - w:SEQ], ALU.add), t_add)
                c.step(nc.vector.tensor_tensor(lg[:, i, 0:w], lg[:, i, 0:w], selp[:, t, 0:w], ALU.add))
                c.step(nc.vector.tensor_reduce(mx[:, i, 1:2], lg[:, i, 0:w], AX.X, ALU.max, negate=True), t_max)
                if n >= 1:
                    normalise(n - 1)
                if n >= GQ + 1 and (n - 1) % GQ == 0:
                    merge((n - 1) // GQ - 1)
            normalise(len(heads) - 1)
            merge(2 * TILES - 1)
            for g in range(2):
                dve.wait_ge(t_sl, g + 1)
                c.step(nc.vector.tensor_reduce(mx[:, g, 1:2], SPAN(2 + 3 * g, 0, TW), AX.X, ALU.max, negate=True), t_smax)
            for g in range(2):
                dve.wait_ge(t_sexp, g + 1)
                c.step(nc.vector.reciprocal(mx[:, g, 3:4], mx[:, g, 2:3]))
                c.step(nc.vector.tensor_scalar(ps_s[:, g, :], ps_s[:, g, :], mx[:, g, 3:4], None, ALU.mult), t_snorm)
            dve.wait_ge(t_vu, NB)
            for g in range(2):
                mt = mtmp[:, :, 0:ST]
                c.step(nc.vector.tensor_tensor(mt, bank(6 + g, P).rearrange("p (t r) -> p r t", r=GQ), gb_s[:, GQ * g:GQ * g + GQ, SEQ:N], ALU.mult))
                m = mg_s[:, GQ * g:GQ * g + GQ, SEQ:N]
                c.step(nc.vector.tensor_tensor(m, m, mt, ALU.add))

    next_stage()
    base_e = base_c
    cur[0] = base_b + H * N * 4
    x1 = place("x1", [P, TILES + 1, D])
    h2 = place("h2", [P, TILES + 1, D])
    JS = TOPK * 2
    JALL = TILES * PH * TOPK + JS
    eid = place("eid", [P, JALL], I32)
    gate = place("gate", [P, JALL])
    keep_end = cur[0]
    wo_b = place("wo_b", [P, KD, D])
    h2T = place("h2T", [P, KD, N])
    vec = place("vec", [P, 5, D])
    xn = place("xn", [P, D])
    top_end = cur[0]
    QR = 2
    spans[:] = [[base_a, base_b], [top_end, 229344]]
    wq_b = fresh("wq_b", [P, QR, KD, 512])
    vecs = fresh("vecs", [ST, 3, D])
    ymid = fresh("ymid", [P, D])
    skT = fresh("skT", [P, 2, PK])
    sk = fresh("sk", [P, 2, PK])
    stats = fresh("stats", [P, 2, 6])
    mv = fresh("mv", [P, 4])
    cur[0] = where_wo = keep_end
    s_all = sb("s_all", [P, TILES, 2 * PH, PK], F32, where_wo)
    cur[0] = keep_end + KD * D * 4 + KD * N * 4
    qT = place("qT", [P, 2, N])
    s_smp = place("s_smp", [P, 4, PK])
    assert cur[0] <= top_end
    i16 = fresh("i16", [P, TILES + 1, 2 * PH, TOPK], U32)
    w16 = fresh("w16", [P, TILES + 1, 2 * PH, TOPK])
    pk = fresh("pk", [P, PK])
    spans.append([where["wq_b"], where["wq_b"] + 4 * QR * KD * 512])
    cand = fresh("cand", [P, PH, TOPK * TOPK])
    oneh = fresh("oneh", [P, PH * TOPK, TOPK])
    i16f = fresh("i16f", [P, 2 * PH, TOPK])
    top = fresh("top", [P, PH * TOPK])
    pos = fresh("pos", [P, PH * TOPK], U32)
    posh = fresh("posh", [P, 2, PH * TOPK], U32)
    posf = fresh("posf", [P, 2, PH * TOPK])
    pick = fresh("pick", [P, 2, PH * TOPK])
    zs = fresh("zs", [P, 2, PH])
    iota16 = fresh("iota16", [P, TOPK])
    u_wo, u_wq0, u_wq1, u_x, u_vec, u_vecs, u_sk, u_one, u_chain, u_y, u_yr, u_var, u_std, u_xn = (sem(f"u_{k}") for k in
        ("wo", "wq0", "wq1", "x", "vec", "vecs", "sk", "one", "chain", "y", "yr", "var", "std", "xn"))
    u_h2, u_tr, u_h2T, u_skt, u_skc, u_q, u_qT, u_s, u_sr, u_sall, u_e, u_ex, u_rep, u_pchain, u_it, u_ssall = (sem(f"u_{k}") for k in
        ("h2", "tr", "h2T", "skt", "skc", "q", "qT", "s", "sr", "sall", "e", "ex", "rep", "pchain", "it", "ssall"))
    rowsof = lambda t: P if t < TILES else ST
    with nc.Block() as block:
        @block.sync
        def _(sp):
            sp.dma_start(wo_b[:, :, :], dap(a["w_out"], 0, [[D, P], [P * D, KD], [1, D]])).then_inc(u_wo, 16)
            sp.dma_start(x1[:, 0:TILES, :], dap(a["x_prompt"], 0, [[D, P], [P * D, TILES], [1, D]])).then_inc(u_x, 16)
            sp.dma_start(x1[0:ST, TILES, :], dap(a["x_sample"], 0, [[D, ST], [1, D]])).then_inc(u_x, 16)
            for j, v in enumerate((dap(a["ln1_g"], 0, [[0, P], [1, D]]), dap(a["ln1_b"], 0, [[0, P], [1, D]]),
                                   *(dap(mod_d, m * D, [[0, P], [1, D]]) for m in (G1, SH2, SC2)))):
                sp.dma_start(vec[:, j, :], v).then_inc(u_vec, 16)
            for j, m in enumerate((G1, SH2, SC2)):
                for b in range(NB):
                    sp.dma_start(vecs[NS * b:NS * b + NS, j, :], dap(mod_d, (1 + b) * 6 * D + m * D, [[0, NS], [1, D]])).then_inc(u_vecs, 16)
            for c in range(2):
                sp.dma_start(sk[:, c, :], dap(a["peer_sub_keys"], c * PK * P, [[P, PK], [1, P]])).then_inc(u_sk, 16)
            sp.dma_start(iota16[:, :], a["iota16"]).then_inc(u_it, 16)
            for n in range(4):
                s = (u_wq0, u_wq1)[n % QR]
                if n >= QR:
                    sp.wait_ge(u_q, 4 * (n - QR + 1))
                sp.dma_start(wq_b[:, n % QR, :, :], dap(a["w_peer_q"], 512 * n, [[2048, P], [P * 2048, KD], [1, 512]])).then_inc(s, 16)
            sp.wait_ge(u_h2, TILES + 1)
            for g in range(1, P // ST):
                sp.dma_start(h2[ST * g:ST * g + ST, TILES, :], h2[0:ST, TILES, :]).then_inc(u_rep, 16)
            sp.wait_ge(u_rep, 48)
            sp.wait_ge(u_it, 16)

        @block.gpsimd
        def _(pool):
            c = Counts(pool, u_pchain)
            pool.wait_ge(u_vec, 80)
            pool.wait_ge(u_vecs, 16 * 24)
            c.step(nc.gpsimd.tensor_scalar(vec[:, 4, :], vec[:, 4, :], 1.0, None, ALU.add))
            c.step(nc.gpsimd.tensor_scalar(vecs[:, 2, :], vecs[:, 2, :], 1.0, None, ALU.add))
            for t in range(TILES + 1):
                r = rowsof(t)
                sc, sh = (vec[:, 4, :], vec[:, 3, :]) if t < TILES else (vecs[:, 2, :], vecs[:, 1, :])
                pool.wait_ge(u_xn, t + 1)
                c.step(nc.gpsimd.tensor_tensor(h2[0:r, t, :], x1[0:r, t, :], sc, ALU.mult))
                c.step(nc.gpsimd.tensor_tensor(h2[0:r, t, :], h2[0:r, t, :], sh, ALU.add), u_h2)

        def half_scores(pe, n):
            pe.wait_ge(u_qT, n + 1)
            if n >= 2:
                pe.wait_ge(u_sall, n - 1)
            g, slot = (n // 2) // 2, 2 * ((n // 2) % 2) + n % 2
            for t in range(TILES):
                nc.tensor.matmul(bank(4 + n % 2, PK, P, PK * t), qT[:, n % 2, P * t:P * t + P], skT[:, n % 2, :], start=True, stop=True)
            nc.tensor.matmul(PS[ST * g:ST * g + ST, 512 * 6 + PK * slot:512 * 6 + PK * slot + PK], qT[:, n % 2, SEQ:N], skT[:, n % 2, :],
                             start=True, stop=True).then_inc(u_s, 1)

        @block.tensor
        def _(pe):
            pe.wait_ge(u_sk, 32)
            for c in range(2):
                last = nc.tensor.transpose(bank(6, P, P, P * c), sk[:, c, :], ident[:, :])
            last.then_inc(u_skt, 1)
            pe.wait_ge(u_wo, 16)

            def y(t):
                r = rowsof(t)
                if t >= 2:
                    pe.wait_ge(u_yr, t - 1)
                for half in range(2):
                    for k in range(KD):
                        last = nc.tensor.matmul(bank(2 * (t % 2) + half, 512, r), mg_s[:, k, P * t:P * t + r],
                                                wo_b[:, k, 512 * half:512 * half + 512], start=k == 0, stop=k == KD - 1)
                last.then_inc(u_y, 1)

            def flip(t):
                r = rowsof(t)
                pe.wait_ge(u_h2, t + 1)
                if t >= 1:
                    pe.wait_ge(u_h2T, t)
                for k in range(KD):
                    last = nc.tensor.transpose(SPAN(4, P * k, P * k + r), h2[0:r, t, P * k:P * k + P], ident[0:r, 0:r])
                last.then_inc(u_tr, 1)

            y(0)
            y(1)
            for t in range(TILES + 1):
                if t + 2 <= TILES:
                    y(t + 2)
                flip(t)
            pe.wait_ge(u_h2T, TILES + 1)
            pe.wait_ge(u_yr, TILES + 1)
            pe.wait_ge(u_skc, 1)
            for n in range(2 * PH):
                if n % 4 == 0:
                    pe.wait_ge((u_wq0, u_wq1)[(n // 4) % QR], 16 * (n // 4 // QR + 1))
                if n >= 2:
                    pe.wait_ge(u_qT, n - 1)
                b0 = 2 * (n % 2)
                for k in range(KD):
                    w = wq_b[:, (n // 4) % QR, k, P * (n % 4):P * (n % 4) + P]
                    fl = dict(start=k == 0, stop=k == KD - 1)
                    nc.tensor.matmul(bank(b0), w, h2T[:, k, 0:SEQ], **fl)
                    last = nc.tensor.matmul(bank(b0 + 1, ST), w, h2T[:, k, SEQ:N], **fl)
                last.then_inc(u_q, 1)
                if n >= 1:
                    half_scores(pe, n - 1)
            half_scores(pe, 2 * PH - 1)

        @block.scalar
        def _(act):
            act.wait_ge(u_skt, 1)
            nc.scalar.activation(skT[:, :, :], bank(6, 2 * PK).rearrange("p (c k) -> p c k", k=PK), ACT.Copy).then_inc(u_skc, 1)
            for t in range(TILES + 1):
                r = rowsof(t)
                act.wait_ge(u_var, t + 1)
                nc.scalar.activation(mv[0:r, 3:4], mv[0:r, 2:3], ACT.Sqrt).then_inc(u_std, 1)
                act.wait_ge(u_tr, t + 1)
                nc.scalar.activation(h2T[:, :, P * t:P * t + r], SPAN(4, 0, D).rearrange("p (k t) -> p k t", t=P)[:, :, 0:r], ACT.Copy).then_inc(u_h2T, 1)
            for n in range(2 * PH):
                act.wait_ge(u_q, n + 1)
                if n >= 2:
                    act.wait_ge(u_s, n - 1)
                nc.scalar.activation(qT[:, n % 2, :], SPAN(2 * (n % 2), 0, N), ACT.Copy).then_inc(u_qT, 1)
                act.wait_ge(u_s, n + 1)
                nc.scalar.activation(s_all[:, :, n, :], bank(4 + n % 2).rearrange("p (t k) -> p t k", k=PK), ACT.Copy).then_inc(u_sall, 1)
            nc.scalar.activation(s_smp[:, :, :], bank(6).rearrange("p (s k) -> p s k", k=PK), ACT.Copy).then_inc(u_ssall, 1)
            for t in range(TILES + 1):
                cols = gate[:, 128 * t:128 * t + (128 if t < TILES else JS)]
                act.wait_ge(u_e, t + 1)
                nc.scalar.activation(cols, cols, ACT.Exp).then_inc(u_ex, 1)

        @block.vector
        def _(dve):
            c = Counts(dve, u_chain)
            dve.wait_ge(u_x, 32)
            dve.wait_ge(u_vec, 80)
            dve.wait_ge(u_vecs, 16 * 24)
            for t in range(TILES + 1):
                r = rowsof(t)
                x = x1[0:r, t, :]
                dve.wait_ge(u_y, t + 1)
                g1 = vec[:, 2, :] if t < TILES else vecs[:, 0, :]
                c.step(nc.vector.tensor_tensor(ymid[0:r, :], SPAN(2 * (t % 2), 0, D, r), g1, ALU.mult), u_yr)
                c.step(nc.vector.scalar_tensor_tensor(x, x, ALPHA, ymid[0:r, :], ALU.mult, ALU.add))
                for j in range(2):
                    c.step(nc.vector.bn_stats(stats[0:r, j, :], x[:, 512 * j:512 * j + 512]))
                c.step(nc.vector.bn_aggr(mv[0:r, 0:2], stats[0:r, :, :]))
                c.step(nc.vector.tensor_scalar(mv[0:r, 2:3], mv[0:r, 1:2], 1e-5, None, ALU.add))
                c.step(nc.vector.reciprocal(mv[0:r, 2:3], mv[0:r, 2:3]), u_var)
                dve.wait_ge(u_std, t + 1)
                c.step(nc.vector.tensor_scalar(x, x, mv[0:r, 0:1], mv[0:r, 3:4], ALU.subtract, ALU.mult))
                c.step(nc.vector.tensor_tensor(x, x, vec[0:r, 0, :], ALU.mult))
                c.step(nc.vector.tensor_tensor(x, x, vec[0:r, 1, :], ALU.add), u_xn)

            def top16(vals, idx, src, scratch):
                c.step(nc.vector.max(vals[:, 0:8], src))
                c.step(nc.vector.max_index(idx[:, 0:8], vals[:, 0:8], src))
                c.step(nc.vector.match_replace(scratch, vals[:, 0:8], src, MARK))
                c.step(nc.vector.max(vals[:, 8:16], scratch))
                c.step(nc.vector.max_index(idx[:, 8:16], vals[:, 8:16], scratch))

            for n in range(2 * PH):
                dve.wait_ge(u_sall, n + 1)
                for t in range(TILES):
                    top16(w16[:, t, n, :], i16[:, t, n, :], s_all[:, t, n, :], pk[:, :])
            dve.wait_ge(u_ssall, 1)
            for n in range(4):
                top16(w16[:, TILES, n, :], i16[:, TILES, n, :], s_smp[:, n, :], pk[:, :])
            dve.wait_ge(u_it, 16)
            dve.wait_ge(u_q, 2 * PH)
            for t in range(TILES + 1):
                nh = PH if t < TILES else 2
                ne = nh * TOPK
                val = w16[:, t, 0:2 * nh, :].rearrange("p (h c) k -> p h c k", c=2)
                idf = i16f[:, 0:2 * nh, :].rearrange("p (h c) k -> p h c k", c=2)
                c.step(nc.vector.tensor_copy(i16f[:, 0:2 * nh, :], i16[:, t, 0:2 * nh, :]))
                shape = [P, nh, TOPK, TOPK]
                c.step(nc.vector.tensor_tensor(cand[:, 0:nh, :].rearrange("p h (a b) -> p h a b", b=TOPK),
                                               val[:, :, 0, :].unsqueeze(3).to_broadcast(shape), val[:, :, 1, :].unsqueeze(2).to_broadcast(shape), ALU.add))
                for h in range(nh):
                    e = slice(TOPK * h, TOPK * h + TOPK)
                    top16(top[:, e], pos[:, e], cand[:, h, :], cand[:, h, :])
                c.step(nc.vector.tensor_single_scalar(posh[:, 0, 0:ne], pos[:, 0:ne], 4, ALU.logical_shift_right))
                c.step(nc.vector.tensor_single_scalar(posh[:, 1, 0:ne], pos[:, 0:ne], TOPK - 1, ALU.bitwise_and))
                c.step(nc.vector.tensor_copy(posf[:, :, 0:ne], posh[:, :, 0:ne]))
                one = oneh[:, 0:ne, :]
                for j in range(2):
                    c.step(nc.vector.tensor_tensor(one, posf[:, j, 0:ne].unsqueeze(2).to_broadcast([P, ne, TOPK]),
                                                   iota16[:, :].unsqueeze(1).to_broadcast([P, ne, TOPK]), ALU.is_equal))
                    one4 = one.rearrange("p (h e) k -> p h e k", e=TOPK)
                    c.step(nc.vector.tensor_tensor(one4, one4, idf[:, :, j, :].unsqueeze(2).to_broadcast(shape), ALU.mult))
                    c.step(nc.vector.tensor_reduce(pick[:, j, 0:ne], one, AX.X, ALU.add))
                at = slice(128 * t, 128 * t + ne)
                c.step(nc.vector.scalar_tensor_tensor(eid[:, at], pick[:, 0, 0:ne], float(PK), pick[:, 1, 0:ne], ALU.mult, ALU.add))
                top3 = top[:, 0:ne].rearrange("p (h e) -> p h e", e=TOPK)
                g3 = gate[:, at].rearrange("p (h e) -> p h e", e=TOPK)
                c.step(nc.vector.tensor_tensor(g3, top3, top3[:, :, 0:1].to_broadcast([P, nh, TOPK]), ALU.subtract), u_e)
                dve.wait_ge(u_ex, t + 1)
                c.step(nc.vector.tensor_reduce(zs[:, 0, 0:nh], g3, AX.X, ALU.add))
                c.step(nc.vector.reciprocal(zs[:, 1, 0:nh], zs[:, 0, 0:nh]))
                c.step(nc.vector.tensor_tensor(g3, g3, zs[:, 1, 0:nh].unsqueeze(2).to_broadcast([P, nh, TOPK]), ALU.mult))

    next_stage()
    spans[:] = [[base_a, base_b + H * N * 4], [keep_end, 229344]]
    UR, VR = 12, 12
    ur = fresh("ur", [P, UR, D])
    vr = fresh("vr", [P, VR, D])
    vec2 = fresh("vec2", [P, 3, D])
    acc = fresh("acc", [P, 2, D])
    g2s = fresh("g2s", [ST, D])
    junk = fresh("junk", [P, D])
    fold2 = fresh("fold2", [P, ST])
    dots = fresh("dots", [P, 2, GROUP])
    acts = fresh("acts", [P, 2, GROUP])
    wts = fresh("wts", [P, GROUP])
    stats2 = fresh("stats2", [P, 2, 6])
    mv2 = fresh("mv2", [P, 4])
    NG = JALL // GROUP
    GT = PH * TOPK // GROUP
    e_u = [sem(f"e_u{i}") for i in range(UR)]
    e_v = [sem(f"e_v{i}") for i in range(VR)]
    e_in, e_chain, e_dot, e_act, e_vdone, e_accd, e_fold, e_var, e_std, e_fin, e_out, e_sfin = (sem(f"e_{k}") for k in
        ("in", "chain", "dot", "act", "vdone", "accd", "fold", "var", "std", "fin", "out", "sfin"))
    with nc.Block() as block:
        @block.sync
        def _(sp):
            for j, v in enumerate((dap(a["ln2_g"], 0, [[0, P], [1, D]]), dap(a["ln2_b"], 0, [[0, P], [1, D]]), dap(mod_d, G2 * D, [[0, P], [1, D]]))):
                sp.dma_start(vec2[:, j, :], v).then_inc(e_in, 16)
            for b in range(NB):
                sp.dma_start(g2s[NS * b:NS * b + NS, :], dap(mod_d, (1 + b) * 6 * D + G2 * D, [[0, NS], [1, D]])).then_inc(e_in, 16)
            sp.dma_start(fold2[:, :], a["fold"]).then_inc(e_in, 16)
            for t in range(TILES):
                sp.wait_ge(e_fin, t + 1)
                sp.dma_start(dap(o["y_prompt"], P * t * D, [[D, P], [1, D]]), x1[:, t, :]).then_inc(e_out, 16)
            sp.wait_ge(e_fin, TILES + 1)
            sp.dma_start(dap(o["y_sample"], 0, [[D, ST], [1, D]]), x1[0:ST, TILES, :]).then_inc(e_out, 16)
            sp.wait_ge(e_out, 16 * (TILES + 1))

        @block.gpsimd
        def _(pool):
            def gather(dst, name, j, s):
                nc.gpsimd.indirect_dma_start(out=dst, out_offset=None, in_=dap(a[name], 0, [[D, PK * PK], [1, D]]),
                                             in_offset=bass.IndirectOffsetOnAxis(eid[:, j:j + 1], 0)).then_inc(s, 16)
            for q in range(NG):
                for j in range(GROUP * q, GROUP * q + GROUP):
                    if j >= UR:
                        pool.wait_ge(e_dot, j - UR + 1)
                    gather(ur[:, j % UR, :], "peer_u", j, e_u[j % UR])
                for j in range(GROUP * q, GROUP * q + GROUP):
                    if j >= VR:
                        pool.wait_ge(e_vdone, j - VR + 1)
                    gather(vr[:, j % VR, :], "peer_v", j, e_v[j % VR])

        @block.scalar
        def _(act):
            for q in range(NG):
                act.wait_ge(e_dot, GROUP * (q + 1))
                if q >= 2:
                    act.wait_ge(e_vdone, GROUP * (q - 1))
                nc.scalar.activation(acts[:, q % 2, :], dots[:, q % 2, :], ACT.Gelu).then_inc(e_act, 1)
                if q >= 1 and q % GT == 0 or q == NG - 1:
                    t = (q - 1) // GT if q < NG - 1 else TILES
                    r = rowsof(t)
                    act.wait_ge(e_var, t + 1)
                    nc.scalar.activation(mv2[0:r, 3:4], mv2[0:r, 2:3], ACT.Sqrt).then_inc(e_std, 1)

        @block.tensor
        def _(pe):
            pe.wait_ge(e_in, 16 * 12)
            pe.wait_ge(e_accd, 1)
            for half in range(2):
                last = nc.tensor.matmul(bank(half, 512, ST), fold2[:, :], acc[:, TILES % 2, 512 * half:512 * half + 512], start=True, stop=True)
            last.then_inc(e_fold, 1)

        @block.vector
        def _(dve):
            c = Counts(dve, e_chain)
            dve.wait_ge(e_in, 16 * 12)

            def add_values(q):
                t = q // GT
                i = t % 2
                dve.wait_ge(e_act, q + 1)
                c.step(nc.vector.tensor_tensor(wts[:, :], acts[:, q % 2, :], gate[:, GROUP * q:GROUP * q + GROUP], ALU.mult))
                for k in range(GROUP):
                    j = GROUP * q + k
                    dve.wait_ge(e_v[j % VR], 16 * (j // VR + 1))
                    if q % GT == 0 and k == 0:
                        c.step(nc.vector.tensor_scalar(acc[:, i, :], vr[:, j % VR, :], wts[:, k:k + 1], None, ALU.mult), e_vdone)
                    else:
                        c.step(nc.vector.scalar_tensor_tensor(acc[:, i, :], vr[:, j % VR, :], wts[:, k:k + 1], acc[:, i, :], ALU.mult, ALU.add), e_vdone)

            def finish(t):
                r = rowsof(t)
                x, ff = x1[0:r, t, :], acc[0:r, t % 2, :]
                if t == TILES:
                    c.step(nc.vector.memset(mv2[:, 0:1], 0.0), e_accd)
                    dve.wait_ge(e_fold, 1)
                    c.step(nc.vector.tensor_tensor(ff, SPAN(0, 0, D, ST), g2s[:, :], ALU.mult))
                else:
                    c.step(nc.vector.tensor_tensor(ff, ff, vec2[:, 2, :], ALU.mult))
                c.step(nc.vector.scalar_tensor_tensor(x, x, ALPHA, ff, ALU.mult, ALU.add))
                for j in range(2):
                    c.step(nc.vector.bn_stats(stats2[0:r, j, :], x[:, 512 * j:512 * j + 512]))
                c.step(nc.vector.bn_aggr(mv2[0:r, 0:2], stats2[0:r, :, :]))
                c.step(nc.vector.tensor_scalar(mv2[0:r, 2:3], mv2[0:r, 1:2], 1e-5, None, ALU.add))
                c.step(nc.vector.reciprocal(mv2[0:r, 2:3], mv2[0:r, 2:3]), e_var)
                dve.wait_ge(e_std, t + 1)
                c.step(nc.vector.tensor_scalar(x, x, mv2[0:r, 0:1], mv2[0:r, 3:4], ALU.subtract, ALU.mult))
                c.step(nc.vector.tensor_tensor(x, x, vec2[0:r, 0, :], ALU.mult))
                c.step(nc.vector.tensor_tensor(x, x, vec2[0:r, 1, :], ALU.add), e_fin)

            for q in range(NG):
                t = q // GT
                for k in range(GROUP):
                    j = GROUP * q + k
                    dve.wait_ge(e_u[j % UR], 16 * (j // UR + 1))
                    c.step(nc.vector.tensor_tensor_reduce(out=junk[:, :], in0=ur[:, j % UR, :], in1=h2[:, t, :], scale=1.0, scalar=0.0,
                                                          op0=ALU.mult, op1=ALU.add, accum_out=dots[:, q % 2, k:k + 1]), e_dot)
                if q >= 1:
                    add_values(q - 1)
                    if q % GT == 0:
                        finish(q // GT - 1)
            add_values(NG - 1)
            finish(TILES)

    es.close()


_INS = ["x_prompt", "x_sample", "cache_k", "cache_v", "cache_kidx", "state_hgrn", "page_table", "c_prompt", "c_sample",
        "w_ada", "b_ada", "w_in", "lb_param", "a_gnorm", "t5_table", "w_out", "ln1_g", "ln1_b", "w_peer_q",
        "peer_sub_keys", "peer_u", "peer_v", "ln2_g", "ln2_b"]
_OUTS = {"y_prompt": (1, SEQ, D), "y_sample": (NB, NS, D), "k_prompt": (1, 1, SEQ, 2, P), "v_prompt": (1, 1, SEQ, 2, P),
         "kidx_prompt": (1, 1, SEQ, ID), "s_prompt": (1, 1, H, P, P), "k_sample": (1, NB, NS, 2, P),
         "v_sample": (1, NB, NS, 2, P), "kidx_sample": (1, NB, NS, ID), "s_sample": (1, NB, H, P, P)}


def kernel(**inputs):
    import concourse.bacc as bacc
    from concourse.bass_utils import run_bass_kernel_spmd

    nc = bacc.Bacc("TRN2", target_bir_lowering=False, num_devices=1)
    arrays, ins, outs = {}, {}, {}
    consts = constants()
    for name in _INS + list(consts):
        arr = np.ascontiguousarray(consts[name] if name in consts else inputs[name])
        arrays[f"in_{name}"] = arr
        ins[name] = nc.dram_tensor(f"in_{name}", arr.shape, mybir.dt.from_np(arr.dtype), kind="ExternalInput").ap()
    ins["c_prompt"] = ins["c_prompt"]
    for name, shape in _OUTS.items():
        outs[name] = nc.dram_tensor(f"out_{name}", shape, F32, kind="ExternalOutput").ap()
    program(nc, ins, outs)
    r = run_bass_kernel_spmd(nc, [arrays], core_ids=[0])
    return tuple(r.results[0][f"out_{name}"] for name in _OUTS)
```

```python
import math
from contextlib import ExitStack

import numpy as np
import concourse.bass as bass
from concourse import mybir

F32 = mybir.dt.float32
U32 = mybir.dt.uint32
I32 = mybir.dt.int32
ALU = mybir.AluOpType
ACT = mybir.ActivationFunctionType
AX = mybir.AxisListType

P = 128
D = 1024
KD = D // P
SEQ = 512
TILES = SEQ // P
NB, NS = 8, 4
ST = NB * NS
N = SEQ + ST
PAST, PAGE = 1024, 128
PAGES = PAST // PAGE
H = 8
GQ = 4
CH = 32
NCH = SEQ // CH
IH, ID = 4, 64
KSEL_P, KSEL_S = 128, 256
TW = PAST + ST
ALPHA = 2.0 ** 0.25
NEG = -1e30
MARK = -3e38
COLS = {"qa": 0, "fa": 1024, "ia": 2048, "ga": 3072, "qb": 4096, "kv": 5120, "ix": 5632, "gate_a": 5956, "gate_b": 6980}
WIN = 8004
SH1, SC1, G1, SH2, SC2, G2 = range(6)
PH, PK, TOPK = 8, 128, 16
GROUP = 4
UR, VR = 8, 8


def dap(ap, offset, pattern):
    return bass.AP(ap.tensor, ap.offset + offset, pattern)


def constants():
    def bucket(rel):
        rel = np.maximum(rel, 0)
        relf = np.maximum(rel, 1).astype(np.float32)
        large = 16 + (np.log(relf / np.float32(16)) / np.float32(math.log(8)) * np.float32(16)).astype(np.int32)
        return np.where(rel < 16, rel, np.minimum(large, 31))
    c = {}
    c["ident"] = np.eye(P)
    c["meanmat"] = np.full((P, P), 1.0 / P)
    s, t = np.arange(CH)[:, None], np.arange(CH)[None]
    tri = (s <= t)
    own = (s // NS == t // NS)
    big = np.arange(P)
    c["chunkmask"] = (big[:, None] <= big[None]) & (big[:, None] // CH == big[None] // CH)
    c["seqmask"] = tri & own
    c["ownchunk"] = big[:, None] // CH == np.arange(P // CH)[None]
    keep = np.ones(N)
    keep[0:SEQ:CH] = 0
    keep[SEQ::NS] = 0
    c["keep"] = np.tile(keep, (P, 1))
    c["ownseq"] = np.arange(ST)[:, None] // NS == np.arange(NB)[None]
    c["causal"] = np.where(np.arange(P)[None] <= np.arange(P)[:, None], 0, NEG)
    c["newmask"] = np.where(tri.T & own.T, 0, NEG)
    c["t5p"] = (np.arange(32)[:, None] == bucket(511 - np.arange(640))[None])
    key = np.concatenate([np.arange(PAST), PAST + np.arange(ST) % NS])
    oh = [(np.arange(32)[:, None] == bucket(PAST + i - key)[None]) for i in range(NS)]
    c["t5s"] = np.concatenate(oh, 0)
    row = np.arange(P)
    c["rowq"] = (row[:, None] // 32 == (row[None] // GQ) % NS)
    c["expand"] = (np.arange(ST)[:, None] == row[None] // GQ)
    c["fold"] = (row[:, None] % ST == np.arange(ST)[None])
    c["iota16"] = np.tile(np.arange(TOPK), (P, 1))
    c["iotap"] = row[:, None]
    return {k: np.ascontiguousarray(v.astype(np.float32)) for k, v in c.items()}


class Counts:
    def __init__(self, eng, chain):
        self.eng, self.chain, self.n = eng, chain, {}

    def step(self, ins, sem=None):
        sem = sem or self.chain
        key = id(sem)
        self.n[key] = self.n.get(key, 0) + 1
        ins.then_inc(sem, 1)
        self.eng.wait_ge(sem, self.n[key])


def program(nc, a, o):
    es = ExitStack()
    live = []

    def sb(name, shape, dt, at):
        t = nc.alloc_sbuf_tensor_at(name, shape, dt, offset=at)
        return t

    stores = {name: nc.alloc_semaphore(name) for name in ("p_out", "r_out0", "r_out1", "e_out")}
    stores.update({f"s_wb{i}": nc.alloc_semaphore(f"s_wb{i}") for i in range(3)})

    def sem(name):
        if name in stores:
            return stores[name]
        live.append(nc.alloc_semaphore(name))
        return live[-1]

    def next_stage():
        nc.clear_and_free_semaphores(live)
        nc.all_engine_barrier()
        live.clear()

    BASE = 16512
    cur = [BASE]

    def place(name, shape, dt=F32):
        at = cur[0]
        cur[0] += -(-int(np.prod(shape[1:])) * 4 // 32) * 32
        assert cur[0] <= 229344, (name, cur[0])
        return sb(name, shape, dt, at)

    PS = es.enter_context(nc.psum_tensor("PS", [P, 8 * 512], F32))

    def bank(i, w=512, p=P, off=0):
        return PS[0:p, 512 * i + off:512 * i + off + w]

    mod_d = nc.dram_tensor("mod_d", [1 + NB, 6 * D], F32, kind="Internal").ap()
    t5_d = nc.dram_tensor("t5_d", [H, 640], F32, kind="Internal").ap()
    t5x_d = nc.dram_tensor("t5x_d", [P, H, 640], F32, kind="Internal").ap()
    h2s_d = nc.dram_tensor("h2s_d", [ST, D], F32, kind="Internal").ap()

    ident = place("ident", [P, P])
    base_a = cur[0]
    q_s = place("q_s", [P, H, N])
    sn_s = place("sn_s", [P, H, N])
    v_s = place("v_s", [P, TILES + 1, D])
    base_b = cur[0]
    mg_s = place("mg_s", [P, H, N])
    gb_s = place("gb_s", [P, H, N])
    qb_s = place("qb_s", [P, H, N])
    kv_s = place("kv_s", [P, TILES + 1, 512])
    qi_s = place("qi_s", [ID, IH, N])
    ki_s = place("ki_s", [ID, N])
    kw_s = place("kw_s", [P, TILES + 1, ID + IH])
    base_c = cur[0]
    hT = place("hT", [P, KD, N])
    base_d = cur[0]

    WR = 3
    wb = place("wb", [P, WR, KD, 512])
    cur[0] = base_a
    c9 = place("c9", [1 + NB, D])
    cT = place("cT", [P, KD, 1 + NB])
    bada = place("bada", [1 + NB, 6 * D])
    modr = place("modr", [1 + NB, 6 * D])
    modT = place("modT", [P, 2 * KD, 1 + NB])
    xt = place("xt", [P, TILES + 1, D])
    htmp = place("htmp", [P, ST])
    w_ada_b = place("w_ada_b", [P, WR, KD, 512])
    assert cur[0] <= base_c, (cur[0], base_c)
    chunks = [("qa", 0, 512), ("qa", 512, 512), ("ga", 0, 512), ("ga", 512, 512), ("fa", 0, 512), ("fa", 512, 512),
              ("gate_a", 0, 512), ("gate_a", 512, 512), ("gate_b", 0, 512), ("gate_b", 512, 512),
              ("qb", 0, 512), ("qb", 512, 512), ("kv", 0, 512), ("ix", 0, 324), ("ia", 0, 512), ("ia", 512, 512)]
    s_wb = [sem(f"s_wb{i}") for i in range(WR)]

    def load_w_in(sp, n):
        name, off, w = chunks[n]
        src = dap(a["w_in"], COLS[name] + off, [[WIN, P], [P * WIN, KD], [1, w]])
        sp.dma_start(wb[:, n % WR, :, 0:w], src).then_inc(s_wb[n % WR], 16)

    s_c, s_x, s_id, s_ba = sem("s_c"), sem("s_x"), sem("s_id"), sem("s_ba")
    s_wa = [sem(f"s_wa{i}") for i in range(WR)]
    m_ct, m_ctready, m_ps, m_row, m_tr, m_xt, m_h, m_chain, m_out = (sem(f"m_{k}") for k in
        ("ct", "ctready", "ps", "row", "tr", "xt", "h", "chain", "out"))
    m_modT = sem("m_modT")
    with nc.Block() as block:
        @block.sync
        def _(sp):
            sp.dma_start(ident[:, :], a["ident"]).then_inc(s_id, 16)
            sp.dma_start(c9[0:1, :], a["c_prompt"]).then_inc(s_c, 16)
            sp.dma_start(c9[1:1 + NB, :], a["c_sample"]).then_inc(s_c, 16)
            sp.dma_start(bada[:, :], dap(a["b_ada"], 0, [[0, 1 + NB], [1, 6 * D]])).then_inc(s_ba, 16)
            for n in range(12):
                if n >= WR:
                    sp.wait_ge(m_ps, n - WR + 1)
                src = dap(a["w_ada"], n * 512, [[6 * D, P], [P * 6 * D, KD], [1, 512]])
                sp.dma_start(w_ada_b[:, n % WR, :, :], src).then_inc(s_wa[n % WR], 16)
            for n in range(WR):
                load_w_in(sp, n)
            sp.wait_ge(m_row, 12)
            sp.dma_start(mod_d, modr[:, :]).then_inc(m_out, 16)
            sp.wait_ge(m_out, 16)

        @block.gpsimd
        def _(pool):
            pool.dma_start(xt[:, 0:TILES, :], dap(a["x_prompt"], 0, [[D, P], [P * D, TILES], [1, D]])).then_inc(s_x, 16)
            pool.dma_start(xt[0:ST, TILES, :], dap(a["x_sample"], 0, [[D, ST], [1, D]])).then_inc(s_x, 16)
            pool.wait_ge(s_x, 32)

        @block.tensor
        def _(pe):
            pe.wait_ge(s_id, 16)
            pe.wait_ge(s_c, 32)
            for k in range(KD):
                last = nc.tensor.transpose(bank(0, 9, P, 16 * k), c9[:, P * k:P * k + P], ident[0:9, 0:9])
            last.then_inc(m_ct, 1)
            pe.wait_ge(m_ctready, 1)
            for n in range(12):
                pe.wait_ge(s_wa[n % WR], 16 * (n // WR + 1))
                if n >= 2:
                    pe.wait_ge(m_row, n - 1)
                for k in range(KD):
                    last = nc.tensor.matmul(bank(1 + n % 2, 512, 9), cT[:, k, :], w_ada_b[:, n % WR, k, :],
                                            start=k == 0, stop=k == KD - 1)
                last.then_inc(m_ps, 1)
                if n == 4:
                    for k in range(2 * KD):
                        pe.wait_ge(m_row, 4)
                        last = nc.tensor.transpose(bank(3, 9, P, 16 * k), modr[:, P * k:P * k + P], ident[0:9, 0:9])
                    last.then_inc(m_tr, 1)
                    pe.wait_ge(s_x, 32)
                    for k in range(KD):
                        if k >= 2:
                            pe.wait_ge(m_h, k - 1)
                        for t in range(TILES):
                            nc.tensor.transpose(bank(4 + k % 2, P, P, P * t), xt[:, t, P * k:P * k + P], ident[:, :])
                        nc.tensor.transpose(bank(6 + k % 2, ST), xt[0:ST, TILES, P * k:P * k + P],
                                            ident[0:ST, 0:ST]).then_inc(m_xt, 1)

        @block.scalar
        def _(act):
            act.wait_ge(m_ct, 1)
            for k in range(KD):
                last = nc.scalar.activation(cT[:, k, :], bank(0, 9, P, 16 * k), ACT.Silu)
            last.then_inc(m_ctready, 1)

        @block.vector
        def _(dve):
            c = Counts(dve, m_chain)
            dve.wait_ge(s_ba, 16)

            def row(n):
                dve.wait_ge(m_ps, n + 1)
                c.step(nc.vector.tensor_tensor(modr[:, 512 * n:512 * n + 512], bank(1 + n % 2, 512, 9),
                                               bada[:, 512 * n:512 * n + 512], ALU.add), m_row)
            for n in range(5):
                row(n)
            dve.wait_ge(m_tr, 1)
            src = bank(3, 256).rearrange("p (k c) -> p k c", c=16)[:, :, 0:9]
            c.step(nc.vector.tensor_copy(modT[:, :, :], src))
            c.step(nc.vector.tensor_scalar(modT[:, KD:2 * KD, :], modT[:, KD:2 * KD, :], 1.0, None, ALU.add))
            for k in range(KD):
                dve.wait_ge(m_xt, k + 1)
                c.step(nc.vector.tensor_scalar(hT[:, k, 0:SEQ], bank(4 + k % 2), modT[:, KD + k, 0:1],
                                               modT[:, k, 0:1], ALU.mult, ALU.add))
                seq3 = lambda ap: ap.rearrange("p (b i) -> p b i", i=NS)
                by_seq = lambda j: modT[:, j, 1:9].unsqueeze(2).to_broadcast([P, NB, NS])
                c.step(nc.vector.tensor_tensor(seq3(htmp[:, :]), seq3(bank(6 + k % 2, ST)), by_seq(KD + k), ALU.mult))
                c.step(nc.vector.tensor_tensor(seq3(hT[:, k, SEQ:N]), seq3(htmp[:, :]), by_seq(k), ALU.add), m_h)
            for n in range(5, 12):
                row(n)

    next_stage()
    cur[0] = base_d + WR * KD * 512 * 4
    sg = place("sg", [P, 2, N])
    units = []
    for n, (name, off, _) in enumerate(chunks):
        if name in ("kv", "ia"):
            units += [(n, name, t) for t in range(TILES + 1)]
        elif name == "ix":
            units += [(n, "qi", h) for h in range(IH)] + [(n, "ki", 0)] + [(n, "kw", t) for t in range(TILES + 1)]
        else:
            units += [(n, name, j) for j in range(4)]
    SLOTS = 4
    p_unit, p_chain, p_sg, p_sgused, p_out, p_achain = (sem(f"p_{k}") for k in
        ("unit", "chain", "sg", "sgused", "out", "achain"))
    p_free = [sem(f"p_free{i}") for i in range(SLOTS)]
    p_kvdone, p_kwdone = sem("p_kvdone"), sem("p_kwdone")
    with nc.Block() as block:
        @block.sync
        def _(sp):
            for n in range(WR, len(chunks)):
                sp.wait_ge(p_unit, sum(1 for x in units if x[0] <= n - WR))
                load_w_in(sp, n)
            sp.wait_ge(p_kvdone, TILES + 1)
            for j, (po, so) in enumerate((("k_prompt", "k_sample"), ("v_prompt", "v_sample"))):
                sp.dma_start(dap(o[po], 0, [[256, P], [P * 256, TILES], [1, 256]]),
                             kv_s[:, 0:TILES, 256 * j:256 * j + 256]).then_inc(p_out, 16)
                sp.dma_start(dap(o[so], 0, [[256, ST], [1, 256]]), kv_s[0:ST, TILES, 256 * j:256 * j + 256]).then_inc(p_out, 16)
            sp.wait_ge(p_kwdone, TILES + 1)
            sp.dma_start(dap(o["kidx_prompt"], 0, [[ID, P], [P * ID, TILES], [1, ID]]), kw_s[:, 0:TILES, 0:ID]).then_inc(p_out, 16)
            sp.dma_start(dap(o["kidx_sample"], 0, [[ID, ST], [1, ID]]), kw_s[0:ST, TILES, 0:ID]).then_inc(p_out, 16)
            sp.wait_ge(p_out, 96)

        @block.tensor
        def _(pe):
            seen = -1
            for u, (n, kind, j) in enumerate(units):
                if n != seen:
                    pe.wait_ge(s_wb[n % WR], 16 * (n // WR + 1))
                    seen = n
                if u >= SLOTS:
                    pe.wait_ge(p_free[u % SLOTS], u // SLOTS)
                b0 = 2 * (u % SLOTS)
                for k in range(KD):
                    w = wb[:, n % WR, k, :]
                    fl = dict(start=k == 0, stop=k == KD - 1)
                    if kind in ("kv", "ia", "kw"):
                        lo, m = P * j, P if j < TILES else ST
                        rhs = w[:, 256:256 + ID + IH] if kind == "kw" else w
                        last = nc.tensor.matmul(bank(b0, ID + IH if kind == "kw" else 512, m), hT[:, k, lo:lo + m], rhs, **fl)
                    else:
                        m = ID if kind in ("qi", "ki") else P
                        lo = 256 if kind == "ki" else m * j
                        for half in range(2):
                            last = nc.tensor.matmul(bank(b0 + half, N // 2, m), w[:, lo:lo + m],
                                                    hT[:, k, N // 2 * half:N // 2 * (half + 1)], **fl)
                last.then_inc(p_unit, 1)

        def src(u, p=P, w=N):
            b0 = 2 * (u % SLOTS)
            if w == N:
                return PS[0:p, 512 * b0:512 * b0 + 1024].rearrange("p (b c) -> p b c", c=512)[:, :, 0:N // 2]
            return PS[0:p, 512 * b0:512 * b0 + w]

        tok2 = lambda ap: ap.rearrange("p (b c) -> p b c", c=N // 2)

        @block.scalar
        def _(act):
            c = Counts(act, p_achain)
            for u, (n, kind, j) in enumerate(units):
                if kind not in ("qa", "ga", "fa", "gate_a", "gate_b"):
                    continue
                h = 4 * (chunks[n][1] // 512) + j
                act.wait_ge(p_unit, u + 1)
                free = p_free[u % SLOTS]
                if kind == "qa":
                    nc.scalar.activation(tok2(q_s[:, h, :]), src(u), ACT.Silu).then_inc(free, 1)
                elif kind == "ga":
                    nc.scalar.activation(tok2(mg_s[:, h, :]), src(u), ACT.Silu).then_inc(free, 1)
                elif kind == "fa":
                    nc.scalar.activation(tok2(sn_s[:, h, :]), src(u), ACT.Sigmoid, scale=-1.0).then_inc(free, 1)
                elif kind == "gate_b":
                    nc.scalar.activation(tok2(gb_s[:, h, :]), src(u), ACT.Sigmoid).then_inc(free, 1)
                else:
                    if h >= 2:
                        act.wait_ge(p_sgused, h - 1)
                    nc.scalar.activation(tok2(sg[:, h % 2, :]), src(u), ACT.Sigmoid).then_inc(p_sg, 1)
                    act.wait_ge(p_sg, h + 1)
                    act.sem_inc(free, 1)

        @block.vector
        def _(dve):
            c = Counts(dve, p_chain)
            for u, (n, kind, j) in enumerate(units):
                if kind in ("qa", "ga", "fa", "gate_b"):
                    continue
                half = chunks[n][1] // 512
                free = p_free[u % SLOTS]
                if kind == "gate_a":
                    h = 4 * half + j
                    dve.wait_ge(p_sg, h + 1)
                    nc.vector.tensor_tensor(mg_s[:, h, :], mg_s[:, h, :], sg[:, h % 2, :], ALU.mult).then_inc(p_sgused, 1)
                    continue
                dve.wait_ge(p_unit, u + 1)
                m = P if j < TILES else ST
                if kind == "qb":
                    nc.vector.tensor_scalar(tok2(qb_s[:, 4 * half + j, :]), src(u), float(P) ** -0.5, None, ALU.mult).then_inc(free, 1)
                elif kind == "qi":
                    nc.vector.tensor_copy(tok2(qi_s[:, j, :]), src(u, ID)).then_inc(free, 1)
                elif kind == "ki":
                    nc.vector.tensor_copy(tok2(ki_s[:, :]), src(u, ID)).then_inc(free, 1)
                elif kind == "ia":
                    nc.vector.tensor_copy(v_s[0:m, j, 512 * half:512 * half + 512], src(u, m, 512)).then_inc(free, 1)
                elif kind == "kv":
                    c.step(nc.vector.tensor_copy(kv_s[0:m, j, :], src(u, m, 512)), p_kvdone)
                    dve.sem_inc(free, 1)
                elif kind == "kw":
                    c.step(nc.vector.tensor_copy(kw_s[0:m, j, :], src(u, m, ID + IH)), p_kwdone)
                    dve.sem_inc(free, 1)

    next_stage()
    cur[0] = base_c
    ab = place("ab", [P, 2, N])
    bc = place("bc", [P, 2, N])
    eb = place("eb", [P, 2, N])
    ke = place("ke", [P, 2, N])
    kd_t = place("kd_t", [P, 2, TILES + 1, P])
    scm = place("scm", [P, 2, SEQ + CH])
    st = place("st", [P, 2, NCH + 1, P])
    s0 = place("s0", [P, 2, NB, P])
    vm = place("vm", [ST, NB, P])
    sn_new = place("sn_new", [P, 2, NB, P])
    sq = place("sq", [P, N])
    rstd = place("rstd", [P, N])
    keep = place("keep", [P, N])
    cmask = place("cmask", [P, P])
    smask = place("smask", [ST, CH])
    ownchunk = place("ownchunk", [P, P // CH])
    vc = place("vc", [P, TILES, P // CH, P])
    ownseq = place("ownseq", [ST, NB])
    meanm = place("meanm", [P, P])
    lbp = place("lbp", [P, 2, H])
    lbm = place("lbm", [P, 3, H])
    gn = place("gn", [P, 1])
    eps6 = place("eps6", [P, 1])
    r_vc = sem("r_vc")
    r_lnms, r_rstd = sem("r_lnms"), sem("r_rstd")
    r_in, r_own, r_chain, r_sm, r_lb, r_ln, r_scan, r_exp, r_d, r_ed, r_prep, r_sc, r_scm, r_kdp, r_kdt, r_ds, r_st, r_dss, r_o, r_sq, r_ms, r_mg, r_vm, r_snew, r_ones = (
        sem(f"r_{k}") for k in ("in", "own", "chain", "sm", "lb", "ln", "scan", "exp", "d", "ed", "prep", "sc", "scm", "kdp", "kdt",
                                "ds", "st", "dss", "o", "sq", "ms", "mg", "vm", "snew", "ones"))
    r_s0 = [sem(f"r_s0{i}") for i in range(2)]
    r_out = [sem(f"r_out{i}") for i in range(2)]
    r_lbd = sem("r_lbd")
    chunks3 = lambda ap: ap[:, 0:SEQ].rearrange("p (c t) -> p c t", t=CH)
    seqs3 = lambda ap: ap[:, SEQ:N].rearrange("p (b t) -> p b t", t=NS)
    with nc.Block() as block:
        def store(sp, h):
            sp.wait_ge(r_st, NCH * (h + 1))
            sp.dma_start(dap(o["s_prompt"], h * P * P, [[P, P], [1, P]]), st[:, h % 2, NCH, :]).then_inc(r_out[h % 2], 16)
            sp.wait_ge(r_snew, 2 * (h + 1))
            sp.dma_start(dap(o["s_sample"], h * P * P, [[P, P], [H * P * P, NB], [1, P]]), sn_new[:, h % 2, :, :]).then_inc(r_out[h % 2], 16)

        @block.sync
        def _(sp):
            for dst, name in ((keep, "keep"), (cmask, "chunkmask"), (meanm, "meanmat"), (smask, "seqmask")):
                sp.dma_start(dst[:, :], a[name]).then_inc(r_in, 16)
            sp.dma_start(ownseq[:, :], a["ownseq"]).then_inc(r_own, 16)
            sp.dma_start(ownchunk[:, :], a["ownchunk"]).then_inc(r_own, 16)
            sp.dma_start(gn[:, :], dap(a["a_gnorm"], 0, [[1, P], [1, 1]])).then_inc(r_in, 16)
            for h in range(H):
                if h >= 2:
                    sp.wait_ge(r_mg, h - 1)
                    sp.wait_ge(r_snew, 2 * (h - 1))
                sp.dma_start(s0[:, h % 2, :, :], dap(a["state_hgrn"], h * P * P, [[P, P], [H * P * P, NB], [1, P]])).then_inc(r_s0[h % 2], 16)
                if h >= 1:
                    store(sp, h - 1)
            store(sp, H - 1)
            sp.wait_ge(r_out[0], 16 * H)
            sp.wait_ge(r_out[1], 16 * H)

        @block.gpsimd
        def _(pool):
            for j in range(2):
                pool.dma_start(lbp[:, j, :], dap(a["lb_param"], j * D, [[1, P], [P, H]]), allow_slow_non_contiguous=True).then_inc(r_lbd, 16)
            pool.wait_ge(r_own, 32)
            for h in range(H):
                for t in range(TILES):
                    if h >= 1:
                        pool.wait_ge(r_ds, TILES * (h - 1) + t + 1)
                    nc.gpsimd.tensor_tensor(vc[:, t, :, :], v_s[:, t, P * h:P * h + P].unsqueeze(1).to_broadcast([P, P // CH, P]),
                                            ownchunk[:, :].unsqueeze(2).to_broadcast([P, P // CH, P]), ALU.mult).then_inc(r_vc, 1)
                if h >= 1:
                    pool.wait_ge(r_dss, 2 * h)
                nc.gpsimd.tensor_tensor(vm[:, :, :], v_s[0:ST, TILES, P * h:P * h + P].unsqueeze(1).to_broadcast([ST, NB, P]),
                                        ownseq[:, :].unsqueeze(2).to_broadcast([ST, NB, P]), ALU.mult).then_inc(r_vm, 1)
            pool.wait_ge(r_lbd, 32)

        @block.scalar
        def _(act):
            act.wait_ge(r_sm, 1)
            nc.scalar.activation(lbm[:, 0:2, :], lbp[:, :, :], ACT.Exp).then_inc(r_lb, 1)
            act.wait_ge(r_ones, 1)

            def logs(h):
                if h >= 2:
                    act.wait_ge(r_kdt, h - 1)
                    act.wait_ge(r_snew, 2 * (h - 1))
                i = h % 2
                nc.scalar.activation(ab[:, i, :], sn_s[:, h, :], ACT.Ln, scale=lbm[:, 2, h:h + 1], bias=1.0).then_inc(r_ln, 1)
                act.wait_ge(r_scan, h + 1)
                nc.scalar.activation(eb[:, i, :], bc[:, i, :], ACT.Exp).then_inc(r_exp, 1)
                nc.scalar.activation(ke[:, i, :], bc[:, i, :], ACT.Exp, scale=-1.0).then_inc(r_exp, 1)
                act.wait_ge(r_d, h + 1)
                nc.scalar.activation(ab[:, i, :], ab[:, i, :], ACT.Exp).then_inc(r_ed, 1)

            def inverse_root(h):
                act.wait_ge(r_ms, h + 1)
                if h >= 1:
                    act.wait_ge(r_mg, h)
                nc.scalar.activation(rstd[:, :], PS[:, 6 * 512:6 * 512 + N], ACT.Ln, bias=eps6[:, 0:1]).then_inc(r_lnms, 1)
                act.wait_ge(r_lnms, h + 1)
                nc.scalar.activation(rstd[:, :], rstd[:, :], ACT.Exp, scale=-0.5).then_inc(r_rstd, 1)

            logs(0)
            logs(1)
            def kd_out(h):
                act.wait_ge(r_kdp, h + 1)
                if h >= 2:
                    act.wait_ge(r_dss, 2 * (h - 1))
                nc.scalar.activation(kd_t[:, h % 2, 0:TILES, :], bank(0).rearrange("p (t k) -> p t k", k=P), ACT.Copy).then_inc(r_kdt, 1)

            kd_out(0)
            for h in range(H):
                if h >= 1:
                    inverse_root(h - 1)
                if h + 2 < H:
                    logs(h + 2)
                if h + 1 < H:
                    kd_out(h + 1)
                act.wait_ge(r_o, h + 1)
                nc.scalar.activation(sq[:, :], PS[:, 4 * 512:4 * 512 + N], ACT.Square).then_inc(r_sq, 1)
            inverse_root(H - 1)

        @block.vector
        def _(dve):
            c = Counts(dve, r_chain)
            dve.wait_ge(r_in, 80)
            c.step(nc.vector.memset(eps6[:, :], 1e-6))
            dve.wait_ge(r_lbd, 32)
            c.step(nc.vector.tensor_tensor(lbm[:, 2, :], lbp[:, 0, :], lbp[:, 1, :], ALU.max))
            c.step(nc.vector.tensor_tensor(lbp[:, :, :], lbp[:, :, :], lbm[:, 2, :].unsqueeze(1).to_broadcast([P, 2, H]), ALU.subtract), r_sm)
            dve.wait_ge(r_lb, 1)
            c.step(nc.vector.tensor_tensor(lbm[:, 2, :], lbm[:, 0, :], lbm[:, 1, :], ALU.add))
            c.step(nc.vector.reciprocal(lbm[:, 2, :], lbm[:, 2, :]))
            c.step(nc.vector.tensor_tensor(lbm[:, 1, :], lbm[:, 1, :], lbm[:, 2, :], ALU.mult))
            c.step(nc.vector.tensor_scalar(lbm[:, 2, :], lbm[:, 1, :], -1.0, None, ALU.mult), r_ones)

            def prep(h):
                i = h % 2
                dve.wait_ge(r_ln, h + 1)
                nc.vector.tensor_scalar(sn_s[:, h, :], sn_s[:, h, :], lbm[:, 1, h:h + 1], None, ALU.mult)
                c.step(nc.vector.tensor_tensor_scan(bc[:, i, :], keep[:, :], ab[:, i, :], 0.0, ALU.mult, ALU.add), r_scan)
                c.step(nc.vector.tensor_tensor(chunks3(ab[:, i, :]), chunks3(bc[:, i, :])[:, :, CH - 1:CH].to_broadcast([P, NCH, CH]),
                                        chunks3(bc[:, i, :]), ALU.subtract))
                c.step(nc.vector.tensor_tensor(seqs3(ab[:, i, :]), seqs3(bc[:, i, :])[:, :, NS - 1:NS].to_broadcast([P, NB, NS]),
                                               seqs3(bc[:, i, :]), ALU.subtract), r_d)
                dve.wait_ge(r_exp, 2 * (h + 1))
                c.step(nc.vector.tensor_tensor(q_s[:, h, :], q_s[:, h, :], eb[:, i, :], ALU.mult))
                c.step(nc.vector.tensor_tensor(ke[:, i, :], ke[:, i, :], sn_s[:, h, :], ALU.mult))
                dve.wait_ge(r_ed, h + 1)
                c.step(nc.vector.tensor_tensor(ab[:, i, :], ab[:, i, :], sn_s[:, h, :], ALU.mult), r_prep)

            def norm(h):
                dve.wait_ge(r_rstd, h + 1)
                c.step(nc.vector.tensor_tensor(rstd[:, :], rstd[:, :], PS[:, 4 * 512:4 * 512 + N], ALU.mult))
                c.step(nc.vector.scalar_tensor_tensor(mg_s[:, h, :], rstd[:, :], gn[:, 0:1], mg_s[:, h, :], ALU.mult, ALU.mult), r_mg)

            prep(0)
            prep(1)
            for h in range(H):
                i = h % 2
                dve.wait_ge(r_sc, h + 1)
                shape = [P, TILES, P // CH, CH]
                c.step(nc.vector.tensor_tensor(scm[:, i, 0:SEQ].rearrange("p (t c s) -> p t c s", c=P // CH, s=CH),
                                               bank(1, P).rearrange("p (t s) -> p t s", s=CH).unsqueeze(2).to_broadcast(shape),
                                               cmask[:, :].rearrange("p (c s) -> p c s", s=CH).unsqueeze(1).to_broadcast(shape), ALU.mult))
                c.step(nc.vector.tensor_tensor(scm[0:ST, i, SEQ:SEQ + CH], bank(1, CH, ST, P), smask[:, :], ALU.mult))
                c.step(nc.vector.tensor_copy(kd_t[0:ST, i, TILES, :], bank(1, P, ST, 256)), r_scm)
                if h >= 2:
                    dve.wait_ge(r_out[i], 32 * (h // 2))
                for n in range(NCH):
                    t = n // 4
                    if n % 4 == 0:
                        dve.wait_ge(r_ds, TILES * h + t + 1)
                    ds = bank(2 + t % 2, P, P, P * (n % 4))
                    if n == 0:
                        c.step(nc.vector.tensor_copy(st[:, i, 1, :], ds), r_st)
                    else:
                        c.step(nc.vector.scalar_tensor_tensor(st[:, i, n + 1, :], st[:, i, n, :], eb[:, i, CH * n + CH - 1:CH * n + CH],
                                                              ds, ALU.mult, ALU.add), r_st)
                dve.wait_ge(r_s0[i], 16 * (h // 2 + 1))
                last = seqs3(eb[:, i, :])[:, :, NS - 1:NS].to_broadcast([P, NB, P])
                c.step(nc.vector.tensor_tensor(sn_new[:, i, :, :], s0[:, i, :, :], last, ALU.mult))
                for j in range(2):
                    dve.wait_ge(r_dss, 2 * h + j + 1)
                    c.step(nc.vector.tensor_tensor(sn_new[:, i, 4 * j:4 * j + 4, :], sn_new[:, i, 4 * j:4 * j + 4, :],
                                                   bank(2 + j).rearrange("p (b v) -> p b v", v=P), ALU.add), r_snew)
                if h >= 1:
                    norm(h - 1)
                if h + 2 < H:
                    prep(h + 2)
            norm(H - 1)

        @block.tensor
        def _(pe):
            pe.wait_ge(r_in, 80)

            def mean_squares(h):
                pe.wait_ge(r_sq, h + 1)
                if h >= 1:
                    pe.wait_ge(r_lnms, h)
                nc.tensor.matmul(bank(6), meanm[:, :], sq[:, 0:SEQ], start=True, stop=True)
                nc.tensor.matmul(bank(7, ST), meanm[:, :], sq[:, SEQ:N], start=True, stop=True).then_inc(r_ms, 1)

            def scores(h):
                i = h % 2
                pe.wait_ge(r_prep, h + 1)
                if h >= 1:
                    pe.wait_ge(r_scm, h)
                for n in range(NCH):
                    lo = 32 * (n % 4)
                    nc.tensor.matmul(PS[lo:lo + 32, 512 + CH * (n // 4):512 + CH * (n // 4) + CH], ke[:, i, CH * n:CH * n + CH],
                                     q_s[:, h, CH * n:CH * n + CH], start=True, stop=True)
                nc.tensor.matmul(bank(1, CH, ST, P), ke[:, i, SEQ:N], q_s[:, h, SEQ:N], start=True, stop=True)
                nc.tensor.transpose(bank(1, P, ST, 256), ab[:, i, SEQ:N], ident[:, :]).then_inc(r_sc, 1)
                if h >= 1:
                    pe.wait_ge(r_kdt, h)
                for t in range(TILES):
                    last = nc.tensor.transpose(bank(0, P, P, P * t), ab[:, i, P * t:P * t + P], ident[:, :])
                last.then_inc(r_kdp, 1)

            def products(h, first, last):
                pe.wait_ge(r_kdt, h + 1)
                for t in range(first, last):
                    if t >= 2:
                        pe.wait_ge(r_st, NCH * h + 4 * (t - 1))
                    elif h >= 1:
                        pe.wait_ge(r_snew, 2 * h)
                    pe.wait_ge(r_vc, TILES * h + t + 1)
                    nc.tensor.matmul(bank(2 + t % 2), kd_t[:, h % 2, t, :], vc[:, t, :, :], start=True, stop=True).then_inc(r_ds, 1)

            scores(0)
            products(0, 0, 2)
            for h in range(H):
                i = h % 2
                v = lambda t, lo, n: v_s[lo:lo + n, t, P * h:P * h + P]
                products(h, 2, TILES)
                if h >= 1:
                    mean_squares(h - 1)
                pe.wait_ge(r_vm, h + 1)
                pe.wait_ge(r_scm, h + 1)
                for j in range(2):
                    pe.wait_ge(r_st, NCH * h + 12 + 4 * j)
                    nc.tensor.matmul(bank(2 + j), kd_t[0:ST, i, TILES, :], vm[:, 4 * j:4 * j + 4, :], start=True, stop=True).then_inc(r_dss, 1)
                if h + 1 < H:
                    scores(h + 1)
                    products(h + 1, 0, 2)
                if h >= 1:
                    pe.wait_ge(r_mg, h)
                for t in range(TILES):
                    nc.tensor.matmul(bank(4, P, P, P * t), v(t, 0, P), scm[:, i, P * t:P * t + P], start=True, stop=False)
                    for n in range(max(4 * t, 1), 4 * t + 4):
                        nc.tensor.matmul(bank(4, CH, P, CH * n), st[:, i, n, :], q_s[:, h, CH * n:CH * n + CH], start=False,
                                         stop=n == 4 * t + 3)
                pe.wait_ge(r_s0[i], 16 * (h // 2 + 1))
                nc.tensor.matmul(bank(5, ST), v(TILES, 0, ST), scm[0:ST, i, SEQ:SEQ + CH], start=True, stop=False)
                for b in range(NB):
                    last = nc.tensor.matmul(bank(5, NS, P, NS * b), s0[:, i, b, :], q_s[:, h, SEQ + NS * b:SEQ + NS * b + NS],
                                            start=False, stop=b == NB - 1)
                last.then_inc(r_o, 1)
            mean_squares(H - 1)

    next_stage()
    spans, where = [], {}

    def fresh(name, shape, dt=F32):
        size = -(-int(np.prod(shape[1:])) * 4 // 32) * 32
        for s in spans:
            if s[0] + size <= s[1]:
                s[0] += size
                where[name] = s[0] - size
                return sb(name, shape, dt, s[0] - size)
        raise AssertionError((name, size, spans))

    spans[:] = [[base_a, base_b], [base_c, 229344]]
    KR = 3
    kvr = fresh("kvr", [P, KR, PAGES, 256])
    kT_c = fresh("kT_c", [P, 2, PAST])
    bt = fresh("bt", [P, H, SEQ])
    fresh("kx", [P, 2 * PAGES * ID + 2 * PAST])
    kxr = sb("kxr", [P, 2, PAGES, ID], F32, where["kx"])
    kxT = sb("kxT", [ID, 2, PAST], F32, where["kx"] + 4 * 2 * PAGES * ID)
    t5s = fresh("t5s", [P, TW])
    selp = fresh("selp", [P, TILES, SEQ])
    work = fresh("work", [P, SEQ])
    rel = fresh("rel", [P, IH, TW // 2])
    rels = fresh("rels", [P, TW])
    sels = fresh("sels", [ST, TW])
    lg = fresh("lg", [P, 2, SEQ])
    pw = fresh("pw", [P, 2, SEQ])
    pT = fresh("pT", [P, 2, SEQ])
    qpad = fresh("qpad", [P, 2, NB, P])
    qall = fresh("qall", [P, 2, P])
    qipad = fresh("qipad", [ID, NB, IH, ST])
    qiall = fresh("qiall", [ID, P])
    kTp = fresh("kTp", [P, 2, N])
    pTs = sb("pTs", [P, 2, PAGES + 1, P], F32, where["kx"])
    ps_s = sb("ps_s", [P, 2, TW], F32, where["rel"])
    mtmp = fresh("mtmp", [P, GQ, P])
    causal = fresh("causal", [P, P])
    newmask = fresh("newmask", [ST, ST])
    rowq = fresh("rowq", [P, P])
    expand = fresh("expand", [ST, P])
    fold = fresh("fold", [P, ST])
    iotap = fresh("iotap", [P, 1])
    tab = fresh("tab", [P, H])
    t5row = fresh("t5row", [H, 640])
    t5p = fresh("t5p", [32, 640])
    ptab = fresh("ptab", [P, NB * PAGES], I32)
    ptabf = fresh("ptabf", [P, NB * PAGES])
    rows = fresh("rows", [P, NB * PAGES], I32)
    wcol = fresh("wcol", [P, 1])
    tbias = fresh("tbias", [P, 2, P])
    m8 = fresh("m8", [P, 8])
    mx = fresh("mx", [P, 2, 4])
    t_bt0, t_foldr = sem("t_bt0"), sem("t_foldr")
    t_in, t_w, t_pt, t_rows, t_chain, t_row, t_t5, t_bt = (sem(f"t_{k}") for k in ("in", "w", "pt", "rows", "chain", "row", "t5", "bt"))
    t_pad0, t_pad, t_kn, t_knc, t_ix, t_rel, t_acc = (sem(f"t_{k}") for k in ("pad0", "pad", "kn", "knc", "ix", "rel", "acc"))
    t_kxt, t_kxc, t_xs, t_relS, t_relw, t_fold, t_sels = (sem(f"t_{k}") for k in ("kxt", "kxc", "xs", "relS", "relw", "fold", "sels"))
    t_lg, t_add, t_max, t_exp, t_norm, t_tr, t_pT, t_pv, t_merge = (sem(f"t_{k}") for k in
        ("lg", "add", "max", "exp", "norm", "tr", "pT", "pv", "merge"))
    t_kct, t_kcc, t_kcu, t_sl, t_smax, t_sexp, t_snorm, t_str, t_spT, t_spv, t_vu, t_smerge = (sem(f"t_{k}") for k in
        ("kct", "kcc", "kcu", "sl", "smax", "sexp", "snorm", "str", "spT", "spv", "vu", "smerge"))
    t_kx = [sem(f"t_kx{i}") for i in range(2)]
    t_kv = [sem(f"t_kv{i}") for i in range(KR)]
    widths = [P * (t + 1) for t in range(TILES)]
    heads = [(t, h) for t in range(TILES) for h in range(H)]
    SPAN = lambda b0, lo, hi, p=P: PS[0:p, 512 * b0 + lo:512 * b0 + hi]
    pieces = [(0, 512), (512, 1024), (1024, TW)]
    with nc.Block() as block:
        @block.sync
        def _(sp):
            sp.dma_start(ptab[:, :], dap(a["page_table"], 0, [[0, P], [1, NB * PAGES]])).then_inc(t_pt, 16)
            sp.dma_start(iotap[:, :], a["iotap"]).then_inc(t_pt, 16)
            for i in range(NS):
                sp.dma_start(tab[32 * i:32 * i + 32, :], a["t5_table"]).then_inc(t_in, 16)
            for i in range(IH):
                sp.dma_start(wcol[ST * i:ST * i + ST, :], kw_s[0:ST, TILES, ID + i:ID + i + 1]).then_inc(t_w, 16)
            for dst, name in ((t5p, "t5p"), (t5s, "t5s"), (causal, "causal"), (newmask, "newmask"), (rowq, "rowq"), (expand, "expand"), (fold, "fold")):
                sp.dma_start(dst[:, :], a[name]).then_inc(t_in, 16)
            sp.wait_ge(t_row, 2)
            sp.dma_start(t5_d, t5row[:, :]).then_inc(t_t5, 16)
            sp.wait_ge(t_t5, 16)
            sp.dma_start(t5x_d, dap(t5_d, 0, [[0, P], [640, H], [1, 640]])).then_inc(t_t5, 16)
            sp.wait_ge(t_t5, 32)
            sp.dma_start(bt[:, :, :], dap(t5x_d, P - 1, [[H * 640 - 1, P], [640, H], [1, SEQ]])).then_inc(t_bt, 16)
            sp.wait_ge(t_bt, 16)

        @block.gpsimd
        def _(pool):
            nc.gpsimd.memset(qpad[:, :, :, :], 0.0)
            nc.gpsimd.memset(qipad[:, :, :, :], 0.0).then_inc(t_pad0, 1)
            pool.wait_ge(t_rows, 1)
            gather = lambda dst, src, at, s: nc.gpsimd.indirect_dma_start(
                out=dst, out_offset=None, in_=src, in_offset=bass.IndirectOffsetOnAxis(rows[:, at:at + 1], 0)).then_inc(s, 16)
            flat = lambda name, w: dap(a[name], 0, [[w, 80 * PAGE], [1, w]])
            for b in range(NB):
                if b >= 2:
                    pool.wait_ge(t_kxt, b - 1)
                for g in range(PAGES):
                    gather(kxr[:, b % 2, g, :], flat("cache_kidx", ID), b * PAGES + g, t_kx[b % 2])
            for n in range(2 * NB):
                if KR <= n < NB + KR:
                    pool.wait_ge(t_kct, 2 * (n - KR + 1))
                elif n >= NB + KR:
                    pool.wait_ge(t_vu, n - KR - NB + 1)
                for g in range(PAGES):
                    gather(kvr[:, n % KR, g, :], flat("cache_k" if n < NB else "cache_v", 256), (n % NB) * PAGES + g, t_kv[n % KR])

        @block.tensor
        def _(pe):
            pe.wait_ge(t_in, 16 * 11)
            nc.tensor.matmul(bank(0, 512, H), tab[0:32, :], t5p[:, 0:512], start=True, stop=True)
            nc.tensor.matmul(bank(1, 128, H), tab[0:32, :], t5p[:, 512:640], start=True, stop=True).then_inc(t_bt0, 1)
            for g in range(2):
                for t in range(TILES):
                    nc.tensor.transpose(bank(2 + 2 * g, P, P, P * t), kv_s[:, t, P * g:P * g + P], ident[:, :])
                last = nc.tensor.transpose(bank(3 + 2 * g, ST), kv_s[0:ST, TILES, P * g:P * g + P], ident[0:ST, 0:ST])
            last.then_inc(t_kn, 1)
            for n, (t, h) in enumerate([(t, h) for t in range(1, TILES) for h in range(IH)]):
                if n >= 2:
                    pe.wait_ge(t_rel, n - 1)
                else:
                    pe.wait_ge(t_row, 2)
                nc.tensor.matmul(bank(n % 2, widths[t]), qi_s[:, h, P * t:P * t + P], ki_s[:, 0:widths[t]], start=True, stop=True).then_inc(t_ix, 1)
            pe.wait_ge(t_pad, 1)
            pe.wait_ge(t_knc, 2)
            pe.wait_ge(t_rel, 12)
            nc.tensor.matmul(SPAN(2, PAST, TW), qiall[:, :], ki_s[:, SEQ:N], start=True, stop=True)
            for b in range(NB):
                pe.wait_ge(t_kx[b % 2], 16 * PAGES * (b // 2 + 1))
                if b >= 1:
                    pe.wait_ge(t_kxc, b)
                for g in range(PAGES):
                    last = nc.tensor.transpose(SPAN(0, P * g, P * g + P, ID), kxr[:, b % 2, g, :], ident[:, :])
                last.then_inc(t_kxt, 1)
                pe.wait_ge(t_kxc, b + 1)
                for lo, hi in pieces[0:2]:
                    last = nc.tensor.matmul(SPAN(2, lo, hi), qipad[:, b, :, :], kxT[:, b % 2, lo:hi], start=b == 0, stop=b == NB - 1)
            last.then_inc(t_xs, 1)
            pe.wait_ge(t_relw, 1)
            for lo, hi in pieces:
                last = nc.tensor.matmul(SPAN(5, lo, hi, ST), fold[:, :], rels[:, lo:hi], start=True, stop=True)
            last.then_inc(t_fold, 1)

            def flip(n):
                t, h = heads[n]
                pe.wait_ge(t_norm, n + 1)
                if n >= 2:
                    pe.wait_ge(t_pT, n - 1)
                for s in range(t + 1):
                    last = nc.tensor.transpose(bank(2 + n % 2, P, P, P * s), pw[:, n % 2, P * s:P * s + P], ident[:, :])
                last.then_inc(t_tr, 1)

            def weighted(n):
                t, h = heads[n]
                pe.wait_ge(t_pT, n + 1)
                if h % GQ == 0 and n >= 2 * GQ:
                    pe.wait_ge(t_merge, n // GQ - 1)
                for s in range(t + 1):
                    last = nc.tensor.matmul(bank(6 + (n // GQ) % 2, P, P, P * (h % GQ)), kv_s[:, s, 256 + P * (h // GQ):256 + P * (h // GQ) + P],
                                            pT[:, n % 2, P * s:P * s + P], start=s == 0, stop=s == t)
                last.then_inc(t_pv, 1)

            pe.wait_ge(t_foldr, 1)
            for g in range(2):
                for lo, hi in pieces:
                    nc.tensor.matmul(SPAN(2 + 3 * g, lo, hi), tbias[:, g, :], t5s[:, lo:hi], start=True, stop=False)
                nc.tensor.matmul(SPAN(2 + 3 * g, PAST, TW), qall[:, g, :], kTp[:, g, SEQ:N], start=False, stop=False)
            for b in range(NB):
                pe.wait_ge(t_kv[b % KR], 16 * PAGES * (b // KR + 1))
                for g in range(2):
                    if 2 * b + g >= 1:
                        pe.wait_ge(t_kcc, 2 * b + g)
                    for s in range(PAGES):
                        last = nc.tensor.transpose(SPAN(0, P * s, P * s + P), kvr[:, b % KR, s, P * g:P * g + P], ident[:, :])
                    last.then_inc(t_kct, 1)
                    pe.wait_ge(t_kcc, 2 * b + g + 1)
                    for lo, hi in pieces[0:2]:
                        last = nc.tensor.matmul(SPAN(2 + 3 * g, lo, hi), qpad[:, g, b, :], kT_c[:, g, lo:hi], start=False, stop=False)
                    last.then_inc(t_kcu, 1)
            pe.wait_ge(t_sels, 1)
            for g in range(2):
                for lo, hi in pieces:
                    last = nc.tensor.matmul(SPAN(2 + 3 * g, lo, hi), expand[:, :], sels[:, lo:hi], start=False, stop=True)
                last.then_inc(t_sl, 1)
            pe.wait_ge(t_sexp, 2)
            for g in range(2):
                pe.wait_ge(t_snorm, g + 1)
                for s in range(PAGES):
                    nc.tensor.transpose(SPAN(3 * g, P * s, P * s + P), ps_s[:, g, P * s:P * s + P], ident[:, :])
                nc.tensor.transpose(SPAN(3 * g, PAST, PAST + P, ST), ps_s[:, g, PAST:TW], ident[:, :]).then_inc(t_str, 1)
            pe.wait_ge(t_spT, 2)
            for g in range(2):
                nc.tensor.matmul(bank(g, P), kv_s[0:ST, TILES, 256 + P * g:256 + P * g + P], pTs[0:ST, g, PAGES, :], start=True, stop=False)

            def sample_values(b):
                n = NB + b
                pe.wait_ge(t_kv[n % KR], 16 * PAGES * (n // KR + 1))
                for g in range(2):
                    for s in range(PAGES):
                        last = nc.tensor.matmul(bank(g, 16, P, 16 * b), kvr[:, n % KR, s, P * g:P * g + P],
                                                pTs[:, g, s, 16 * b:16 * b + 16], start=False, stop=b == NB - 1 and s == PAGES - 1)
                last.then_inc(t_vu, 1)

            def logits(n):
                t, h = heads[n]
                if n >= 2:
                    pe.wait_ge(t_add, n - 1)
                nc.tensor.matmul(bank(4 + n % 2, widths[t]), qb_s[:, h, P * t:P * t + P], kTp[:, h // GQ, 0:widths[t]],
                                 start=True, stop=True).then_inc(t_lg, 1)

            logits(0)
            logits(1)
            for n in range(len(heads)):
                if n + 2 < len(heads):
                    logits(n + 2)
                flip(n)
                if n >= 1:
                    weighted(n - 1)
                if n % 4 == 3:
                    sample_values(n // 4)
            weighted(len(heads) - 1)

        @block.scalar
        def _(act):
            for n, (t, h) in enumerate([(t, h) for t in range(1, TILES) for h in range(IH)]):
                act.wait_ge(t_ix, n + 1)
                if n >= IH:
                    act.wait_ge(t_acc, n - IH + 1)
                nc.scalar.activation(rel[:, h, 0:widths[t]], bank(n % 2, widths[t]), ACT.Relu, scale=ID ** -0.5).then_inc(t_rel, 1)
            for b in range(NB):
                act.wait_ge(t_kxt, b + 1)
                nc.scalar.activation(kxT[:, b % 2, :], SPAN(0, 0, PAST, ID), ACT.Copy).then_inc(t_kxc, 1)
            act.wait_ge(t_xs, 1)
            nc.scalar.activation(rels[:, :], SPAN(2, 0, TW), ACT.Relu, scale=ID ** -0.5).then_inc(t_relS, 1)

            for n in range(2 * NB):
                act.wait_ge(t_kct, n + 1)
                if n >= 2:
                    act.wait_ge(t_kcu, n - 1)
                nc.scalar.activation(kT_c[:, n % 2, :], SPAN(0, 0, PAST), ACT.Copy).then_inc(t_kcc, 1)
            for g in range(2):
                act.wait_ge(t_smax, g + 1)
                nc.scalar.activation(ps_s[:, g, :], SPAN(2 + 3 * g, 0, TW), ACT.Exp, bias=mx[:, g, 1:2], accum_out=mx[:, g, 2:3]).then_inc(t_sexp, 1)
            for g in range(2):
                act.wait_ge(t_str, g + 1)
                nc.scalar.activation(pTs[:, g, 0:PAGES, :], SPAN(3 * g, 0, PAST).rearrange("p (s r) -> p s r", r=P), ACT.Copy)
                nc.scalar.activation(pTs[0:ST, g, PAGES, :], SPAN(3 * g, PAST, PAST + P, ST), ACT.Copy).then_inc(t_spT, 1)

            def copy_out(n):
                t, h = heads[n]
                act.wait_ge(t_tr, n + 1)
                if n >= 2:
                    act.wait_ge(t_pv, n - 1)
                nc.scalar.activation(pT[:, n % 2, 0:widths[t]], bank(2 + n % 2, widths[t]), ACT.Copy).then_inc(t_pT, 1)

            for n, (t, h) in enumerate(heads):
                act.wait_ge(t_max, n + 1)
                if n >= 2:
                    act.wait_ge(t_tr, n - 1)
                nc.scalar.activation(pw[:, n % 2, 0:widths[t]], lg[:, n % 2, 0:widths[t]], ACT.Exp, bias=mx[:, n % 2, 1:2],
                                     accum_out=mx[:, n % 2, 2:3]).then_inc(t_exp, 1)
                if n >= 1:
                    copy_out(n - 1)
            copy_out(len(heads) - 1)

        @block.vector
        def _(dve):
            c = Counts(dve, t_chain)
            dve.wait_ge(t_pt, 32)
            c.step(nc.vector.tensor_copy(ptabf[:, :], ptab[:, :]))
            c.step(nc.vector.tensor_scalar(rows[:, :], ptabf[:, :], float(PAGE), iotap[:, 0:1], ALU.mult, ALU.add), t_rows)
            dve.wait_ge(t_bt0, 1)
            c.step(nc.vector.tensor_copy(t5row[:, 0:512], bank(0, 512, H)), t_row)
            c.step(nc.vector.tensor_copy(t5row[:, 512:640], bank(1, 128, H)), t_row)
            dve.wait_ge(t_kn, 1)
            for g in range(2):
                c.step(nc.vector.tensor_copy(kTp[:, g, :], SPAN(2 + 2 * g, 0, N)), t_knc)
            dve.wait_ge(t_pad0, 1)
            for b in range(NB):
                c.step(nc.vector.tensor_copy(qipad[:, b, :, NS * b:NS * b + NS], qi_s[:, :, SEQ + NS * b:SEQ + NS * b + NS]))
            c.step(nc.vector.tensor_copy(qiall[:, :].rearrange("p (h t) -> p h t", t=ST), qi_s[:, :, SEQ:N]), t_pad)
            qv = lambda g, b0, b1: qb_s[:, GQ * g:GQ * g + GQ, SEQ + NS * b0:SEQ + NS * b1].rearrange("p r t -> p t r")
            for g in range(2):
                c.step(nc.vector.tensor_copy(qall[:, g, :].rearrange("p (t r) -> p t r", r=GQ), qv(g, 0, NB)))
                for b in range(NB):
                    c.step(nc.vector.tensor_copy(qpad[:, g, b, 16 * b:16 * b + 16].rearrange("p (t r) -> p t r", r=GQ), qv(g, b, b + 1)))
                c.step(nc.vector.tensor_tensor(tbias[:, g, :].rearrange("p (t r) -> p t r", r=GQ), rowq[:, :].rearrange("p (t r) -> p t r", r=GQ),
                                               tab[:, GQ * g:GQ * g + GQ].unsqueeze(1).to_broadcast([P, ST, GQ]), ALU.mult))

            def take_top(w, k):
                for r in range(k // 8):
                    c.step(nc.vector.max(m8[0:w.shape[0], :], w))
                    c.step(nc.vector.match_replace(w, m8[0:w.shape[0], :], w, MARK))

            c.step(nc.vector.tensor_copy(selp[:, 0, 0:P], causal[:, :]))
            for t in range(1, TILES):
                w = work[:, 0:widths[t]]
                for h in range(IH):
                    n = IH * (t - 1) + h
                    wi = kw_s[:, t, ID + h:ID + h + 1]
                    dve.wait_ge(t_rel, n + 1)
                    if h == 0:
                        c.step(nc.vector.tensor_scalar(w, rel[:, h, 0:widths[t]], wi, None, ALU.mult), t_acc)
                    else:
                        c.step(nc.vector.scalar_tensor_tensor(w, rel[:, h, 0:widths[t]], wi, w, ALU.mult, ALU.add), t_acc)
                c.step(nc.vector.tensor_scalar(w, w, IH ** -0.5, None, ALU.mult))
                c.step(nc.vector.tensor_tensor(work[:, P * t:P * t + P], work[:, P * t:P * t + P], causal[:, :], ALU.add))
                take_top(w, KSEL_P)
                c.step(nc.vector.tensor_scalar(selp[:, t, 0:widths[t]], w, MARK, NEG, ALU.not_equal, ALU.mult))
            dve.wait_ge(t_relS, 1)
            dve.wait_ge(t_w, 16 * IH)
            c.step(nc.vector.tensor_scalar(rels[:, :], rels[:, :], wcol[:, 0:1], None, ALU.mult), t_relw)
            dve.wait_ge(t_fold, 1)
            c.step(nc.vector.tensor_scalar(sels[:, :], SPAN(5, 0, TW, ST), IH ** -0.5, None, ALU.mult), t_foldr)
            c.step(nc.vector.tensor_tensor(sels[:, PAST:TW], sels[:, PAST:TW], newmask[:, :], ALU.add))
            take_top(sels[:, :], KSEL_S)
            c.step(nc.vector.tensor_scalar(sels[:, :], sels[:, :], MARK, NEG, ALU.not_equal, ALU.mult), t_sels)

            for g in range(2):
                dve.wait_ge(t_sl, g + 1)
                c.step(nc.vector.tensor_reduce(mx[:, g, 1:2], SPAN(2 + 3 * g, 0, TW), AX.X, ALU.max, negate=True), t_smax)
            for g in range(2):
                dve.wait_ge(t_sexp, g + 1)
                c.step(nc.vector.reciprocal(mx[:, g, 3:4], mx[:, g, 2:3]))
                c.step(nc.vector.tensor_scalar(ps_s[:, g, :], ps_s[:, g, :], mx[:, g, 3:4], None, ALU.mult), t_snorm)

            def normalise(n):
                t, h = heads[n]
                dve.wait_ge(t_exp, n + 1)
                c.step(nc.vector.reciprocal(mx[:, n % 2, 3:4], mx[:, n % 2, 2:3]))
                c.step(nc.vector.tensor_scalar(pw[:, n % 2, 0:widths[t]], pw[:, n % 2, 0:widths[t]], mx[:, n % 2, 3:4], None, ALU.mult), t_norm)

            def merge(q):
                t, g = q // 2, q % 2
                dve.wait_ge(t_pv, GQ * (q + 1))
                c.step(nc.vector.tensor_tensor(mtmp[:, :, :], bank(6 + q % 2).rearrange("p (h t) -> p h t", t=P),
                                               gb_s[:, GQ * g:GQ * g + GQ, P * t:P * t + P], ALU.mult))
                m = mg_s[:, GQ * g:GQ * g + GQ, P * t:P * t + P]
                c.step(nc.vector.tensor_tensor(m, m, mtmp[:, :, :], ALU.add), t_merge)

            dve.wait_ge(t_bt, 16)
            for n, (t, h) in enumerate(heads):
                w = widths[t]
                i = n % 2
                dve.wait_ge(t_lg, n + 1)
                c.step(nc.vector.tensor_tensor(lg[:, i, 0:w], bank(4 + i, w), bt[:, h, SEQ - w:SEQ], ALU.add), t_add)
                c.step(nc.vector.tensor_tensor(lg[:, i, 0:w], lg[:, i, 0:w], selp[:, t, 0:w], ALU.add))
                c.step(nc.vector.tensor_reduce(mx[:, i, 1:2], lg[:, i, 0:w], AX.X, ALU.max, negate=True), t_max)
                if n >= 1:
                    normalise(n - 1)
                if n >= GQ + 2 and (n - 2) % GQ == 0:
                    merge((n - 2) // GQ - 1)
            normalise(len(heads) - 1)
            merge(2 * TILES - 1)
            dve.wait_ge(t_vu, NB)
            for g in range(2):
                mt = mtmp[:, :, 0:ST]
                c.step(nc.vector.tensor_tensor(mt, bank(g, P).rearrange("p (t r) -> p r t", r=GQ), gb_s[:, GQ * g:GQ * g + GQ, SEQ:N], ALU.mult))
                m = mg_s[:, GQ * g:GQ * g + GQ, SEQ:N]
                c.step(nc.vector.tensor_tensor(m, m, mt, ALU.add))

    next_stage()
    cur[0] = base_b + H * N * 4
    x1 = place("x1", [P, TILES + 1, D])
    h2 = place("h2", [P, TILES + 1, D])
    JS = TOPK * 2
    JALL = TILES * PH * TOPK + JS
    eid = place("eid", [P, JALL], I32)
    gate = place("gate", [P, JALL])
    i16 = place("i16", [P, TILES + 1, 2 * PH, TOPK], U32)
    w16 = place("w16", [P, TILES + 1, 2 * PH, TOPK])
    h2T = place("h2T", [P, KD, N])
    skT = place("skT", [P, 2, PK])
    keep_end = cur[0]
    wo_b = place("wo_b", [P, KD, D])
    vec = place("vec", [P, 5, D])
    top_end = cur[0]
    QR = 2
    spans[:] = [[base_a, base_b], [top_end, 229344]]
    wq_b = fresh("wq_b", [P, QR, KD, 512])
    vecs = fresh("vecs", [ST, 3, D])
    ymid = fresh("ymid", [P, D])
    sk = fresh("sk", [P, 2, PK])
    stats = fresh("stats", [P, 2, 6])
    mv = fresh("mv", [P, 4])
    wts0 = fresh("wts0", [P, 1])
    qtok = fresh("qtok", [P, 2, 512])
    qT0 = fresh("qT0", [P, 2, 4, P])
    s0q = fresh("s0q", [P, 2, 4, PK])
    pk = fresh("pk", [P, PK])
    u_wo, u_wq0, u_wq1, u_x, u_vec, u_vecs, u_sk, u_one, u_chain, u_y, u_yr, u_var, u_std, u_xn = (sem(f"u_{k}") for k in
        ("wo", "wq0", "wq1", "x", "vec", "vecs", "sk", "one", "chain", "y", "yr", "var", "std", "xn"))
    u_h2, u_tr, u_h2T, u_skt, u_skc, u_q, u_qT, u_s, u_sr, u_sall, u_e, u_ex, u_rep, u_pchain, u_it, u_ssall = (sem(f"u_{k}") for k in
        ("h2", "tr", "h2T", "skt", "skc", "q", "qT", "s", "sr", "sall", "e", "ex", "rep", "pchain", "it", "ssall"))
    def top16(c, vals, idx, src, scratch):
        c.step(nc.vector.max(vals[:, 0:8], src))
        c.step(nc.vector.max_index(idx[:, 0:8], vals[:, 0:8], src))
        c.step(nc.vector.match_replace(scratch, vals[:, 0:8], src, MARK))
        c.step(nc.vector.max(vals[:, 8:16], scratch))
        c.step(nc.vector.max_index(idx[:, 8:16], vals[:, 8:16], scratch))

    u_qc, u_qtr, u_top = sem("u_qc"), sem("u_qtr"), sem("u_top")
    rowsof = lambda t: P if t < TILES else ST
    with nc.Block() as block:
        @block.sync
        def _(sp):
            sp.dma_start(wo_b[:, :, :], dap(a["w_out"], 0, [[D, P], [P * D, KD], [1, D]])).then_inc(u_wo, 16)
            sp.dma_start(x1[:, 0:TILES, :], dap(a["x_prompt"], 0, [[D, P], [P * D, TILES], [1, D]])).then_inc(u_x, 16)
            sp.dma_start(x1[0:ST, TILES, :], dap(a["x_sample"], 0, [[D, ST], [1, D]])).then_inc(u_x, 16)
            for j, v in enumerate((dap(a["ln1_g"], 0, [[0, P], [1, D]]), dap(a["ln1_b"], 0, [[0, P], [1, D]]),
                                   *(dap(mod_d, m * D, [[0, P], [1, D]]) for m in (G1, SH2, SC2)))):
                sp.dma_start(vec[:, j, :], v).then_inc(u_vec, 16)
            for j, m in enumerate((G1, SH2, SC2)):
                for b in range(NB):
                    sp.dma_start(vecs[NS * b:NS * b + NS, j, :], dap(mod_d, (1 + b) * 6 * D + m * D, [[0, NS], [1, D]])).then_inc(u_vecs, 16)
            for c in range(2):
                sp.dma_start(sk[:, c, :], dap(a["peer_sub_keys"], c * PK * P, [[P, PK], [1, P]])).then_inc(u_sk, 16)
            sp.wait_ge(u_wo, 16)
            for n in range(4):
                s = (u_wq0, u_wq1)[n % QR]
                if n >= QR:
                    sp.wait_ge(u_q, n - QR + 1)
                sp.dma_start(wq_b[:, n % QR, :, :], dap(a["w_peer_q"], 512 * n, [[2048, P], [P * 2048, KD], [1, 512]])).then_inc(s, 16)
            sp.wait_ge(u_h2, TILES + 1)
            for g in range(1, P // ST):
                sp.dma_start(h2[ST * g:ST * g + ST, TILES, :], h2[0:ST, TILES, :]).then_inc(u_rep, 16)
            sp.wait_ge(u_rep, 48)

        @block.gpsimd
        def _(pool):
            c = Counts(pool, u_pchain)
            pool.wait_ge(u_vec, 80)
            pool.wait_ge(u_vecs, 16 * 24)
            c.step(nc.gpsimd.tensor_scalar(vec[:, 4, :], vec[:, 4, :], 1.0, None, ALU.add))
            c.step(nc.gpsimd.tensor_scalar(vecs[:, 2, :], vecs[:, 2, :], 1.0, None, ALU.add))
            for t in range(TILES + 1):
                r = rowsof(t)
                sc, sh = (vec[:, 4, :], vec[:, 3, :]) if t < TILES else (vecs[:, 2, :], vecs[:, 1, :])
                pool.wait_ge(u_xn, t + 1)
                c.step(nc.gpsimd.tensor_tensor(h2[0:r, t, :], x1[0:r, t, :], sc, ALU.mult))
                c.step(nc.gpsimd.tensor_tensor(h2[0:r, t, :], h2[0:r, t, :], sh, ALU.add), u_h2)

        def queries(pe, n):
            pe.wait_ge((u_wq0, u_wq1)[n % QR], 16 * (n // QR + 1))
            if n == 0:
                pe.wait_ge(u_h2T, 1)
                pe.wait_ge(u_skc, 1)
            else:
                pe.wait_ge(u_qc, n)
            for k in range(KD):
                last = nc.tensor.matmul(bank(6), h2T[:, k, 0:P], wq_b[:, n % QR, k, :], start=k == 0, stop=k == KD - 1)
            last.then_inc(u_q, 1)

        def flip_queries(pe, n):
            pe.wait_ge(u_qc, n + 1)
            if n >= 1:
                pe.wait_ge(u_sall, n)
            for j in range(4):
                last = nc.tensor.transpose(bank(7, P, P, P * j), qtok[:, n % 2, P * j:P * j + P], ident[:, :])
            last.then_inc(u_qtr, 1)

        def first_scores(pe, n):
            pe.wait_ge(u_qT, n + 1)
            for j in range(4):
                last = nc.tensor.matmul(bank(7, PK, P, PK * j), qT0[:, n % 2, j, :], skT[:, j % 2, :], start=True, stop=True)
            last.then_inc(u_s, 1)

        @block.tensor
        def _(pe):
            pe.wait_ge(u_sk, 32)
            for c in range(2):
                last = nc.tensor.transpose(bank(6, P, P, P * c), sk[:, c, :], ident[:, :])
            last.then_inc(u_skt, 1)
            pe.wait_ge(u_wo, 16)

            def y(t):
                r = rowsof(t)
                if t >= 2:
                    pe.wait_ge(u_yr, t - 1)
                for half in range(2):
                    for k in range(KD):
                        last = nc.tensor.matmul(bank(2 * (t % 2) + half, 512, r), mg_s[:, k, P * t:P * t + r],
                                                wo_b[:, k, 512 * half:512 * half + 512], start=k == 0, stop=k == KD - 1)
                last.then_inc(u_y, 1)

            def flip(t):
                r = rowsof(t)
                pe.wait_ge(u_h2, t + 1)
                if t >= 1:
                    pe.wait_ge(u_h2T, t)
                for k in range(KD):
                    last = nc.tensor.transpose(SPAN(4, P * k, P * k + r), h2[0:r, t, P * k:P * k + P], ident[0:r, 0:r])
                last.then_inc(u_tr, 1)

            y(0)
            y(1)
            flip(0)
            queries(pe, 0)
            y(2)
            flip_queries(pe, 0)
            for n in range(1, 4):
                queries(pe, n)
                first_scores(pe, n - 1)
                flip(n)
                if n + 2 <= TILES:
                    y(n + 2)
                flip_queries(pe, n)
            first_scores(pe, 3)
            flip(TILES)

        @block.scalar
        def _(act):
            act.wait_ge(u_skt, 1)
            nc.scalar.activation(skT[:, :, :], bank(6, 2 * PK).rearrange("p (c k) -> p c k", k=PK), ACT.Copy).then_inc(u_skc, 1)
            def deviation(t):
                r = rowsof(t)
                act.wait_ge(u_var, t + 1)
                nc.scalar.activation(mv[0:r, 3:4], mv[0:r, 2:3], ACT.Sqrt).then_inc(u_std, 1)

            def h2_out(t):
                r = rowsof(t)
                act.wait_ge(u_tr, t + 1)
                nc.scalar.activation(h2T[:, :, P * t:P * t + r], SPAN(4, 0, D).rearrange("p (k t) -> p k t", t=P)[:, :, 0:r], ACT.Copy).then_inc(u_h2T, 1)

            def queries_out(n):
                act.wait_ge(u_q, n + 1)
                if n >= 2:
                    act.wait_ge(u_qtr, n - 1)
                nc.scalar.activation(qtok[:, n % 2, :], bank(6), ACT.Copy).then_inc(u_qc, 1)

            def flipped_out(n):
                act.wait_ge(u_qtr, n + 1)
                if n >= 2:
                    act.wait_ge(u_s, n - 1)
                nc.scalar.activation(qT0[:, n % 2, :, :], bank(7).rearrange("p (j t) -> p j t", t=P), ACT.Copy).then_inc(u_qT, 1)

            def scores_out(n):
                act.wait_ge(u_s, n + 1)
                if n >= 2:
                    act.wait_ge(u_top, 4 * (n - 1))
                nc.scalar.activation(s0q[:, n % 2, :, :], bank(7).rearrange("p (j k) -> p j k", k=PK), ACT.Copy).then_inc(u_sall, 1)

            deviation(0)
            h2_out(0)
            deviation(1)
            queries_out(0)
            deviation(2)
            flipped_out(0)
            for n in range(1, 4):
                queries_out(n)
                scores_out(n - 1)
                h2_out(n)
                if n + 2 <= TILES:
                    deviation(n + 2)
                flipped_out(n)
            scores_out(3)
            h2_out(TILES)

        @block.vector
        def _(dve):
            c = Counts(dve, u_chain)
            dve.wait_ge(u_x, 32)
            dve.wait_ge(u_vec, 80)
            dve.wait_ge(u_vecs, 16 * 24)
            def norm1(t):
                r = rowsof(t)
                x = x1[0:r, t, :]
                dve.wait_ge(u_y, t + 1)
                g1 = vec[:, 2, :] if t < TILES else vecs[:, 0, :]
                c.step(nc.vector.tensor_tensor(ymid[0:r, :], SPAN(2 * (t % 2), 0, D, r), g1, ALU.mult), u_yr)
                c.step(nc.vector.scalar_tensor_tensor(x, x, ALPHA, ymid[0:r, :], ALU.mult, ALU.add))
                for j in range(2):
                    c.step(nc.vector.bn_stats(stats[0:r, j, :], x[:, 512 * j:512 * j + 512]))
                c.step(nc.vector.bn_aggr(mv[0:r, 0:2], stats[0:r, :, :]))
                c.step(nc.vector.tensor_scalar(mv[0:r, 2:3], mv[0:r, 1:2], 1e-5, None, ALU.add))
                c.step(nc.vector.reciprocal(mv[0:r, 2:3], mv[0:r, 2:3]), u_var)
                dve.wait_ge(u_std, t + 1)
                c.step(nc.vector.tensor_scalar(x, x, mv[0:r, 0:1], mv[0:r, 3:4], ALU.subtract, ALU.mult))
                c.step(nc.vector.tensor_tensor(x, x, vec[0:r, 0, :], ALU.mult))
                c.step(nc.vector.tensor_tensor(x, x, vec[0:r, 1, :], ALU.add), u_xn)

            def search(n):
                dve.wait_ge(u_sall, n + 1)
                for j in range(4):
                    top16(c, w16[:, 0, 4 * n + j, :], i16[:, 0, 4 * n + j, :], s0q[:, n % 2, j, :], pk[:, :])
                    c.step(nc.vector.memset(wts0[:, 0:1], 0.0), u_top)

            norm1(0)
            norm1(1)
            norm1(2)
            for n in range(4):
                search(n)
                if n + 3 <= TILES:
                    norm1(n + 3)

    spans[:] = [[base_a, base_b + H * N * 4], [keep_end, 229344]]
    ur = fresh("ur", [P, UR, D])
    vr = fresh("vr", [P, VR, D])
    vec2 = fresh("vec2", [P, 3, D])
    acc = fresh("acc", [P, 2, D])
    REST = N - P
    wq2 = fresh("wq2", [P, 2, KD, 256])
    g2s = sb("g2s", [ST, D], F32, where["wq2"])
    qTr = fresh("qTr", [P, 2, REST])
    s_r = fresh("s_r", [P, 2, TILES - 1, PK])
    s_smp = fresh("s_smp", [P, 4, PK])
    pk2 = fresh("pk2", [P, PK])
    e_w = [sem(f"e_w{i}") for i in range(2)]
    e_q, e_qc, e_s, e_sc, e_top, e_smp, e_g2 = (sem(f"e_{k}") for k in ("q", "qc", "s", "sc", "top", "smp", "g2"))
    junk = fresh("junk", [P, D])
    fold2 = fresh("fold2", [P, ST])
    cand = fresh("cand", [P, PH, TOPK * TOPK])
    oneh = fresh("oneh", [P, PH * TOPK, TOPK])
    i16f = fresh("i16f", [P, 2 * PH, TOPK])
    top = fresh("top", [P, PH * TOPK])
    pos = fresh("pos", [P, PH * TOPK], U32)
    posh = fresh("posh", [P, 2, PH * TOPK], U32)
    posf = fresh("posf", [P, 2, PH * TOPK])
    pick = fresh("pick", [P, 2, PH * TOPK])
    zs = fresh("zs", [P, 2, PH])
    iota16 = fresh("iota16", [P, TOPK])

    def part(q):
        k = q % GT - 18 if q < GT else q % GT // 2 if q % 2 else -1
        return (q // GT + 1, k) if 0 <= k <= 12 and q // GT < TILES else None
    e_ids, e_g, e_ex = sem("e_ids"), sem("e_g"), sem("e_ex")
    dots = fresh("dots", [P, 2, GROUP])
    acts = fresh("acts", [P, 2, GROUP])
    wts = fresh("wts", [P, GROUP])
    stats2 = fresh("stats2", [P, 2, 6])
    mv2 = fresh("mv2", [P, 4])
    NG = JALL // GROUP
    GT = PH * TOPK // GROUP
    e_u = [sem(f"e_u{i}") for i in range(UR)]
    e_v = [sem(f"e_v{i}") for i in range(VR)]
    e_in, e_chain, e_dot, e_act, e_vdone, e_accd, e_fold, e_var, e_std, e_fin, e_out, e_sfin = (sem(f"e_{k}") for k in
        ("in", "chain", "dot", "act", "vdone", "accd", "fold", "var", "std", "fin", "out", "sfin"))
    with nc.Block() as block:
        @block.sync
        def _(sp):
            for j, v in enumerate((dap(a["ln2_g"], 0, [[0, P], [1, D]]), dap(a["ln2_b"], 0, [[0, P], [1, D]]), dap(mod_d, G2 * D, [[0, P], [1, D]]))):
                sp.dma_start(vec2[:, j, :], v).then_inc(e_in, 16)
            sp.dma_start(fold2[:, :], a["fold"]).then_inc(e_in, 16)
            sp.dma_start(iota16[:, :], a["iota16"]).then_inc(e_in, 16)
            for n in range(8):
                if n >= 2:
                    sp.wait_ge(e_q, 2 * (n - 1))
                sp.dma_start(wq2[:, n % 2, :, :], dap(a["w_peer_q"], 256 * n, [[2048, P], [P * 2048, KD], [1, 256]])).then_inc(e_w[n % 2], 16)
            sp.wait_ge(e_q, 2 * PH)
            for b in range(NB):
                sp.dma_start(g2s[NS * b:NS * b + NS, :], dap(mod_d, (1 + b) * 6 * D + G2 * D, [[0, NS], [1, D]])).then_inc(e_g2, 16)
            for t in range(TILES):
                sp.wait_ge(e_fin, t + 1)
                sp.dma_start(dap(o["y_prompt"], P * t * D, [[D, P], [1, D]]), x1[:, t, :]).then_inc(e_out, 16)
            sp.wait_ge(e_fin, TILES + 1)
            sp.dma_start(dap(o["y_sample"], 0, [[D, ST], [1, D]]), x1[0:ST, TILES, :]).then_inc(e_out, 16)
            sp.wait_ge(e_out, 16 * (TILES + 1))

        @block.gpsimd
        def _(pool):
            def gather(dst, name, j, s):
                nc.gpsimd.indirect_dma_start(out=dst, out_offset=None, in_=dap(a[name], 0, [[D, PK * PK], [1, D]]),
                                             in_offset=bass.IndirectOffsetOnAxis(eid[:, j:j + 1], 0)).then_inc(s, 16)
            for q in range(NG):
                if q % GT == 0:
                    pool.wait_ge(e_ids, q // GT + 1)
                for j in range(GROUP * q, GROUP * q + GROUP):
                    if j >= UR:
                        pool.wait_ge(e_dot, j - UR + 1)
                    gather(ur[:, j % UR, :], "peer_u", j, e_u[j % UR])
                for j in range(GROUP * q, GROUP * q + GROUP):
                    if j >= VR:
                        pool.wait_ge(e_vdone, j - VR + 1)
                    gather(vr[:, j % VR, :], "peer_v", j, e_v[j % VR])

        @block.scalar
        def _(act):
            def gates(t):
                cols = gate[:, 128 * t:128 * t + (128 if t < TILES else JS)]
                act.wait_ge(e_g, t + 1)
                nc.scalar.activation(cols, cols, ACT.Exp).then_inc(e_ex, 1)

            gates(0)
            for q in range(NG):
                if part(q) and part(q)[1] == 12:
                    gates(q // GT + 1)
                act.wait_ge(e_dot, GROUP * (q + 1))
                if q >= 2:
                    act.wait_ge(e_vdone, GROUP * (q - 1))
                nc.scalar.activation(acts[:, q % 2, :], dots[:, q % 2, :], ACT.Gelu).then_inc(e_act, 1)
                if q < 2 * PH:
                    act.wait_ge(e_q, q + 1)
                    if q >= 2:
                        act.wait_ge(e_s, q - 1)
                    nc.scalar.activation(qTr[:, q % 2, :], bank(q % 2, REST), ACT.Copy).then_inc(e_qc, 1)
                if 1 <= q <= 2 * PH:
                    n = q - 1
                    act.wait_ge(e_s, n + 1)
                    if n >= 2:
                        act.wait_ge(e_top, (TILES - 1) * (n - 1))
                    nc.scalar.activation(s_r[:, n % 2, :, :], bank(2 + n % 2, (TILES - 1) * PK).rearrange("p (t k) -> p t k", k=PK),
                                         ACT.Copy).then_inc(e_sc, 1)
                if q == 2 * PH + 1:
                    nc.scalar.activation(s_smp[:, :, :], bank(4).rearrange("p (s k) -> p s k", k=PK), ACT.Copy).then_inc(e_smp, 1)
                if q >= 1 and q % GT == 0 or q == NG - 1:
                    t = (q - 1) // GT if q < NG - 1 else TILES
                    r = rowsof(t)
                    act.wait_ge(e_var, t + 1)
                    nc.scalar.activation(mv2[0:r, 3:4], mv2[0:r, 2:3], ACT.Sqrt).then_inc(e_std, 1)

        @block.tensor
        def _(pe):
            def scores(n):
                pe.wait_ge(e_qc, n + 1)
                if n >= 2:
                    pe.wait_ge(e_sc, n - 1)
                g, slot = (n // 2) // 2, 2 * ((n // 2) % 2) + n % 2
                for t in range(TILES - 1):
                    nc.tensor.matmul(bank(2 + n % 2, PK, P, PK * t), qTr[:, n % 2, P * t:P * t + P], skT[:, n % 2, :], start=True, stop=True)
                nc.tensor.matmul(PS[ST * g:ST * g + ST, 512 * 4 + PK * slot:512 * 4 + PK * slot + PK], qTr[:, n % 2, SEQ - P:REST],
                                 skT[:, n % 2, :], start=True, stop=True).then_inc(e_s, 1)

            for n in range(2 * PH):
                pe.wait_ge(e_w[(n // 2) % 2], 16 * (n // 4 + 1))
                if n >= 2:
                    pe.wait_ge(e_qc, n - 1)
                for k in range(KD):
                    last = nc.tensor.matmul(bank(n % 2, REST), wq2[:, (n // 2) % 2, k, P * (n % 2):P * (n % 2) + P], h2T[:, k, P:N],
                                            start=k == 0, stop=k == KD - 1)
                last.then_inc(e_q, 1)
                if n >= 1:
                    scores(n - 1)
            scores(2 * PH - 1)
            pe.wait_ge(e_in, 16 * 5)
            pe.wait_ge(e_accd, 1)
            for half in range(2):
                last = nc.tensor.matmul(bank(half, 512, ST), fold2[:, :], acc[:, TILES % 2, 512 * half:512 * half + 512], start=True, stop=True)
            last.then_inc(e_fold, 1)

        @block.vector
        def _(dve):
            c = Counts(dve, e_chain)
            dve.wait_ge(e_in, 16 * 5)

            def add_values(q):
                t = q // GT
                i = t % 2
                dve.wait_ge(e_act, q + 1)
                c.step(nc.vector.tensor_tensor(wts[:, :], acts[:, q % 2, :], gate[:, GROUP * q:GROUP * q + GROUP], ALU.mult))
                for k in range(GROUP):
                    j = GROUP * q + k
                    dve.wait_ge(e_v[j % VR], 16 * (j // VR + 1))
                    if q % GT == 0 and k == 0:
                        c.step(nc.vector.tensor_scalar(acc[:, i, :], vr[:, j % VR, :], wts[:, k:k + 1], None, ALU.mult), e_vdone)
                    else:
                        c.step(nc.vector.scalar_tensor_tensor(acc[:, i, :], vr[:, j % VR, :], wts[:, k:k + 1], acc[:, i, :], ALU.mult, ALU.add), e_vdone)

            def finish(t):
                r = rowsof(t)
                x, ff = x1[0:r, t, :], acc[0:r, t % 2, :]
                if t == TILES:
                    c.step(nc.vector.memset(mv2[:, 0:1], 0.0), e_accd)
                    dve.wait_ge(e_fold, 1)
                    dve.wait_ge(e_g2, 16 * NB)
                    c.step(nc.vector.tensor_tensor(ff, SPAN(0, 0, D, ST), g2s[:, :], ALU.mult))
                else:
                    c.step(nc.vector.tensor_tensor(ff, ff, vec2[:, 2, :], ALU.mult))
                c.step(nc.vector.scalar_tensor_tensor(x, x, ALPHA, ff, ALU.mult, ALU.add))
                for j in range(2):
                    c.step(nc.vector.bn_stats(stats2[0:r, j, :], x[:, 512 * j:512 * j + 512]))
                c.step(nc.vector.bn_aggr(mv2[0:r, 0:2], stats2[0:r, :, :]))
                c.step(nc.vector.tensor_scalar(mv2[0:r, 2:3], mv2[0:r, 1:2], 1e-5, None, ALU.add))
                c.step(nc.vector.reciprocal(mv2[0:r, 2:3], mv2[0:r, 2:3]), e_var)
                dve.wait_ge(e_std, t + 1)
                c.step(nc.vector.tensor_scalar(x, x, mv2[0:r, 0:1], mv2[0:r, 3:4], ALU.subtract, ALU.mult))
                c.step(nc.vector.tensor_tensor(x, x, vec2[0:r, 0, :], ALU.mult))
                c.step(nc.vector.tensor_tensor(x, x, vec2[0:r, 1, :], ALU.add), e_fin)

            heads_of = lambda t: PH if t < TILES else 2

            def pairs(t):
                nh = heads_of(t)
                val = w16[:, t, 0:2 * nh, :].rearrange("p (h c) k -> p h c k", c=2)
                c.step(nc.vector.tensor_copy(i16f[:, 0:2 * nh, :], i16[:, t, 0:2 * nh, :]))
                shape = [P, nh, TOPK, TOPK]
                c.step(nc.vector.tensor_tensor(cand[:, 0:nh, :].rearrange("p h (a b) -> p h a b", b=TOPK),
                                               val[:, :, 0, :].unsqueeze(3).to_broadcast(shape), val[:, :, 1, :].unsqueeze(2).to_broadcast(shape), ALU.add))

            def best_pairs(h):
                e = TOPK * h
                for lo in (e, e + 8):
                    c.step(nc.vector.max(top[:, lo:lo + 8], cand[:, h, :]))
                    c.step(nc.vector.max_index(pos[:, lo:lo + 8], top[:, lo:lo + 8], cand[:, h, :]))
                    if lo == e:
                        c.step(nc.vector.match_replace(cand[:, h, :], top[:, lo:lo + 8], cand[:, h, :], MARK))

            def halves(t):
                ne = heads_of(t) * TOPK
                c.step(nc.vector.tensor_single_scalar(posh[:, 0, 0:ne], pos[:, 0:ne], 4, ALU.logical_shift_right))
                c.step(nc.vector.tensor_single_scalar(posh[:, 1, 0:ne], pos[:, 0:ne], TOPK - 1, ALU.bitwise_and))
                c.step(nc.vector.tensor_copy(posf[:, :, 0:ne], posh[:, :, 0:ne]))

            def keys(t, j):
                nh, ne = heads_of(t), heads_of(t) * TOPK
                one = oneh[:, 0:ne, :]
                one4 = one.rearrange("p (h e) k -> p h e k", e=TOPK)
                idf = i16f[:, 0:2 * nh, :].rearrange("p (h c) k -> p h c k", c=2)[:, :, j, :]
                c.step(nc.vector.tensor_tensor(one, posf[:, j, 0:ne].unsqueeze(2).to_broadcast([P, ne, TOPK]),
                                               iota16[:, :].unsqueeze(1).to_broadcast([P, ne, TOPK]), ALU.is_equal))
                c.step(nc.vector.tensor_tensor(one4, one4, idf.unsqueeze(2).to_broadcast([P, nh, TOPK, TOPK]), ALU.mult))
                c.step(nc.vector.tensor_reduce(pick[:, j, 0:ne], one, AX.X, ALU.add))

            def ids_and_gates(t):
                nh, ne = heads_of(t), heads_of(t) * TOPK
                at = slice(128 * t, 128 * t + ne)
                c.step(nc.vector.scalar_tensor_tensor(eid[:, at], pick[:, 0, 0:ne], float(PK), pick[:, 1, 0:ne], ALU.mult, ALU.add), e_ids)
                top3 = top[:, 0:ne].rearrange("p (h e) -> p h e", e=TOPK)
                g3 = gate[:, at].rearrange("p (h e) -> p h e", e=TOPK)
                c.step(nc.vector.tensor_tensor(g3, top3, top3[:, :, 0:1].to_broadcast([P, nh, TOPK]), ALU.subtract), e_g)
                dve.wait_ge(e_ex, t + 1)
                c.step(nc.vector.tensor_reduce(zs[:, 0, 0:nh], g3, AX.X, ALU.add))
                c.step(nc.vector.reciprocal(zs[:, 1, 0:nh], zs[:, 0, 0:nh]))
                c.step(nc.vector.tensor_tensor(g3, g3, zs[:, 1, 0:nh].unsqueeze(2).to_broadcast([P, nh, TOPK]), ALU.mult))

            def choose(t, k):
                if k == 0:
                    pairs(t)
                elif 1 <= k <= heads_of(t):
                    best_pairs(k - 1)
                elif k == 9:
                    halves(t)
                elif k in (10, 11):
                    keys(t, k - 10)
                elif k == 12:
                    ids_and_gates(t)

            for k in range(13):
                choose(0, k)
            for q in range(NG):
                t = q // GT
                if 2 <= q < 2 * PH + 2:
                    dve.wait_ge(e_sc, q - 1)
                    for n in range(TILES - 1):
                        top16(c, w16[:, n + 1, q - 2, :], i16[:, n + 1, q - 2, :], s_r[:, q % 2, n, :], pk2[:, :])
                        c.step(nc.vector.memset(wts[:, 0:1], 0.0), e_top)
                if q == GT:
                    dve.wait_ge(e_smp, 1)
                    for n in range(4):
                        top16(c, w16[:, TILES, n, :], i16[:, TILES, n, :], s_smp[:, n, :], pk2[:, :])
                if part(q):
                    choose(*part(q))
                for k in range(GROUP):
                    j = GROUP * q + k
                    dve.wait_ge(e_u[j % UR], 16 * (j // UR + 1))
                    c.step(nc.vector.tensor_tensor_reduce(out=junk[:, :], in0=ur[:, j % UR, :], in1=h2[:, t, :], scale=1.0, scalar=0.0,
                                                          op0=ALU.mult, op1=ALU.add, accum_out=dots[:, q % 2, k:k + 1]), e_dot)
                if q >= 1:
                    add_values(q - 1)
                    if q % GT == 0:
                        finish(q // GT - 1)
            add_values(NG - 1)
            finish(TILES)

    es.close()


_INS = ["x_prompt", "x_sample", "cache_k", "cache_v", "cache_kidx", "state_hgrn", "page_table", "c_prompt", "c_sample",
        "w_ada", "b_ada", "w_in", "lb_param", "a_gnorm", "t5_table", "w_out", "ln1_g", "ln1_b", "w_peer_q",
        "peer_sub_keys", "peer_u", "peer_v", "ln2_g", "ln2_b"]
_OUTS = {"y_prompt": (1, SEQ, D), "y_sample": (NB, NS, D), "k_prompt": (1, 1, SEQ, 2, P), "v_prompt": (1, 1, SEQ, 2, P),
         "kidx_prompt": (1, 1, SEQ, ID), "s_prompt": (1, 1, H, P, P), "k_sample": (1, NB, NS, 2, P),
         "v_sample": (1, NB, NS, 2, P), "kidx_sample": (1, NB, NS, ID), "s_sample": (1, NB, H, P, P)}


def kernel(**inputs):
    import concourse.bacc as bacc
    from concourse.bass_utils import run_bass_kernel_spmd

    nc = bacc.Bacc("TRN2", target_bir_lowering=False, num_devices=1)
    arrays, ins, outs = {}, {}, {}
    consts = constants()
    for name in _INS + list(consts):
        arr = np.ascontiguousarray(consts[name] if name in consts else inputs[name])
        arrays[f"in_{name}"] = arr
        ins[name] = nc.dram_tensor(f"in_{name}", arr.shape, mybir.dt.from_np(arr.dtype), kind="ExternalInput").ap()
    for name, shape in _OUTS.items():
        outs[name] = nc.dram_tensor(f"out_{name}", shape, F32, kind="ExternalOutput").ap()
    program(nc, ins, outs)
    r = run_bass_kernel_spmd(nc, [arrays], core_ids=[0])
    return tuple(r.results[0][f"out_{name}"] for name in _OUTS)
```
